# Optimizing a Trainium2 kernel written in Bass

```python
import jax, jax.numpy as jnp
from jax import lax
import numpy as np

D_MODEL = 1024
BATCH = 1
SEQ = 1024
DEPTH = 1

LRU_WIDTH = D_MODEL
LRU_HEADS = 8
LRU_HEAD_DIM = LRU_WIDTH // LRU_HEADS
LRU_C = 8.0
CONV_WIDTH = 4
DN_HEADS = 8
DN_HEAD_K = 128
DN_HEAD_V = 128
DN_KEY_DIM = DN_HEADS * DN_HEAD_K
DN_VALUE_DIM = DN_HEADS * DN_HEAD_V
DN_CONV_DIM = 2 * DN_KEY_DIM + DN_VALUE_DIM
CHUNK = 64
D_MIX = LRU_WIDTH + DN_VALUE_DIM
D_IN = 2 * LRU_WIDTH + DN_CONV_DIM + DN_VALUE_DIM + 2 * DN_HEADS
SPLITS = [LRU_WIDTH, 2 * LRU_WIDTH, 2 * LRU_WIDTH + DN_CONV_DIM,
          2 * LRU_WIDTH + DN_CONV_DIM + DN_VALUE_DIM,
          2 * LRU_WIDTH + DN_CONV_DIM + DN_VALUE_DIM + DN_HEADS]
EPS = 1e-6

kernel_name = "hymba_rglru_gated_deltanet_trunk"

def rmsnorm(x, w):
    xf = x.astype(jnp.float32)
    y = xf * lax.rsqrt(jnp.mean(xf * xf, axis=-1, keepdims=True) + EPS)
    return (y * w.astype(jnp.float32)).astype(x.dtype)

def gated_rmsnorm(o, z, w):
    of = o.astype(jnp.float32)
    y = of * lax.rsqrt(jnp.mean(of * of, axis=-1, keepdims=True) + EPS)
    return (y * w.astype(jnp.float32) * jax.nn.silu(z.astype(jnp.float32))).astype(o.dtype)

def l2norm(x):
    return x * lax.rsqrt(jnp.sum(x * x, axis=-1, keepdims=True) + EPS)

def causal_dwconv(x, w):
    K = w.shape[0]
    S = x.shape[1]
    xp = jnp.pad(x, ((0, 0), (K - 1, 0), (0, 0)))
    y = xp[:, 0:S] * w[0]
    for j in range(1, K):
        y = y + xp[:, j:j + S] * w[j]
    return y

def rg_lru(x, wa, ba, wx, bx, lam):
    B_, S_, W = x.shape
    xh = x.reshape(B_, S_, LRU_HEADS, LRU_HEAD_DIM)
    r = jax.nn.sigmoid(jnp.einsum('bshi,hij->bshj', xh, wa).reshape(B_, S_, W) + ba)
    i = jax.nn.sigmoid(jnp.einsum('bshi,hij->bshj', xh, wx).reshape(B_, S_, W) + bx)
    log_a = -LRU_C * r * jax.nn.softplus(-lam)
    a = jnp.exp(log_a)
    mult = jnp.sqrt(-jnp.expm1(2.0 * log_a))
    b = mult * (i * x)

    def combine(left, right):
        a_l, b_l = left
        a_r, b_r = right
        return a_l * a_r, a_r * b_l + b_r

    _, h = lax.associative_scan(combine, (a, b), axis=1)
    return h

def gated_delta_rule(q, k, v, g, beta):
    B_, S_, H, dk = q.shape
    dv = v.shape[-1]
    N = S_ // CHUNK

    def to_chunks(t):
        return t.reshape(B_, N, CHUNK, H, t.shape[-1]).transpose(0, 3, 1, 2, 4)

    q, k, v = to_chunks(q), to_chunks(k), to_chunks(v)
    g = g.reshape(B_, N, CHUNK, H).transpose(0, 3, 1, 2)
    beta = beta.reshape(B_, N, CHUNK, H).transpose(0, 3, 1, 2)
    k_beta = k * beta[..., None]
    v_beta = v * beta[..., None]
    gc = jnp.cumsum(g, axis=-1)
    tri = jnp.tril(jnp.ones((CHUNK, CHUNK), dtype=bool))
    strict = jnp.tril(jnp.ones((CHUNK, CHUNK), dtype=bool), -1)
    decay_mask = jnp.exp(jnp.where(tri, gc[..., :, None] - gc[..., None, :], -jnp.inf))
    A = jnp.where(strict, jnp.einsum('bhncd,bhnjd->bhncj', k_beta, k) * decay_mask, 0.0)
    T = A + jnp.eye(CHUNK, dtype=A.dtype)
    u = lax.linalg.triangular_solve(T, v_beta, left_side=True, lower=True, unit_diagonal=True)
    w = lax.linalg.triangular_solve(T, k_beta * jnp.exp(gc)[..., None],
                                    left_side=True, lower=True, unit_diagonal=True)
    attn = jnp.where(tri, jnp.einsum('bhncd,bhnjd->bhncj', q, k) * decay_mask, 0.0)

    def step(state, xs):
        q_i, k_i, u_i, w_i, attn_i, gc_i = xs
        v_new = u_i - jnp.einsum('bhcd,bhde->bhce', w_i, state)
        o_i = (jnp.einsum('bhcd,bhde->bhce', q_i * jnp.exp(gc_i)[..., None], state)
               + jnp.einsum('bhcj,bhje->bhce', attn_i, v_new))
        g_last = gc_i[..., -1]
        state = (state * jnp.exp(g_last)[..., None, None]
                 + jnp.einsum('bhcd,bhce->bhde', k_i * jnp.exp(g_last[..., None] - gc_i)[..., None], v_new))
        return state, o_i

    xs = tuple(jnp.moveaxis(t, 2, 0) for t in (q, k, u, w, attn, gc))
    state0 = jnp.zeros((B_, H, dk, dv), dtype=q.dtype)
    _, o = lax.scan(step, state0, xs)
    return o.transpose(1, 0, 3, 2, 4).reshape(B_, S_, H, dv)

def hybrid_layer(x, norm_w, w_in, lru_conv_w, lru_conv_b, lru_wa, lru_ba, lru_wx, lru_bx,
                 lru_lambda, lru_norm_w, dn_conv_w, dn_A_log, dn_dt_bias, dn_norm_w, w_out):
    B_, S_, _ = x.shape
    f32 = jnp.float32
    h = rmsnorm(x, norm_w)
    proj = jnp.einsum('bsd,de->bse', h, w_in)
    lru_x, lru_z, dn_qkv, dn_z, dn_b, dn_a = jnp.split(proj, SPLITS, axis=-1)

    xc = (causal_dwconv(lru_x, lru_conv_w) + lru_conv_b).astype(f32)
    hl = rg_lru(xc, lru_wa.astype(f32), lru_ba.astype(f32), lru_wx.astype(f32),
                lru_bx.astype(f32), lru_lambda.astype(f32))
    y_lru = gated_rmsnorm(hl.reshape(B_, S_, LRU_HEADS, LRU_HEAD_DIM),
                          lru_z.reshape(B_, S_, LRU_HEADS, LRU_HEAD_DIM),
                          lru_norm_w.reshape(LRU_HEADS, LRU_HEAD_DIM))

    qkv = jax.nn.silu(causal_dwconv(dn_qkv, dn_conv_w)).astype(f32)
    q, k, v = jnp.split(qkv, [DN_KEY_DIM, 2 * DN_KEY_DIM], axis=-1)
    q = l2norm(q.reshape(B_, S_, DN_HEADS, DN_HEAD_K)) * (DN_HEAD_K ** -0.5)
    k = l2norm(k.reshape(B_, S_, DN_HEADS, DN_HEAD_K))
    v = v.reshape(B_, S_, DN_HEADS, DN_HEAD_V)
    beta = jax.nn.sigmoid(dn_b.astype(f32))
    g = -jnp.exp(dn_A_log.astype(f32)) * jax.nn.softplus(dn_a.astype(f32) + dn_dt_bias.astype(f32))
    o = gated_delta_rule(q, k, v, g, beta)
    y_dn = gated_rmsnorm(o, dn_z.reshape(B_, S_, DN_HEADS, DN_HEAD_V), dn_norm_w)

    y = jnp.concatenate([y_lru.reshape(B_, S_, LRU_WIDTH), y_dn.reshape(B_, S_, DN_VALUE_DIM)],
                        axis=-1).astype(x.dtype)
    return x + jnp.einsum('bse,ed->bsd', y, w_out).astype(x.dtype)

def setup_inputs(seed: int = 0) -> dict:
    key = jax.random.key(seed)
    ks = jax.random.split(key, 20)
    nrm = jax.random.normal
    L = DEPTH
    x = nrm(ks[0], (BATCH, SEQ, D_MODEL), jnp.float32)
    norm_w = 1.0 + 0.01 * nrm(ks[1], (L, D_MODEL), jnp.float32)
    w_in = nrm(ks[2], (L, D_MODEL, D_IN), jnp.float32) * D_MODEL ** -0.5
    lru_conv_w = nrm(ks[3], (L, CONV_WIDTH, LRU_WIDTH), jnp.float32) * CONV_WIDTH ** -0.5
    lru_conv_b = 0.01 * nrm(ks[4], (L, LRU_WIDTH), jnp.float32)
    lru_wa = nrm(ks[5], (L, LRU_HEADS, LRU_HEAD_DIM, LRU_HEAD_DIM), jnp.float32) * LRU_HEAD_DIM ** -0.5
    lru_ba = 0.01 * nrm(ks[6], (L, LRU_WIDTH), jnp.float32)
    lru_wx = nrm(ks[7], (L, LRU_HEADS, LRU_HEAD_DIM, LRU_HEAD_DIM), jnp.float32) * LRU_HEAD_DIM ** -0.5
    lru_bx = 0.01 * nrm(ks[8], (L, LRU_WIDTH), jnp.float32)
    a0 = jax.random.uniform(ks[9], (L, LRU_WIDTH), jnp.float32, 0.9, 0.999)
    s = a0 ** (1.0 / LRU_C)
    lru_lambda = jnp.log(s) - jnp.log1p(-s)
    lru_norm_w = 1.0 + 0.01 * nrm(ks[10], (L, LRU_WIDTH), jnp.float32)
    dn_conv_w = nrm(ks[11], (L, CONV_WIDTH, DN_CONV_DIM), jnp.float32) * CONV_WIDTH ** -0.5
    dn_A_log = jnp.log(jax.random.uniform(ks[12], (L, DN_HEADS), jnp.float32, 1.0, 16.0))
    dt = jnp.exp(jax.random.uniform(ks[13], (L, DN_HEADS), jnp.float32,
                                    float(np.log(1e-3)), float(np.log(1e-1))))
    dn_dt_bias = dt + jnp.log(-jnp.expm1(-dt))
    dn_norm_w = 1.0 + 0.01 * nrm(ks[14], (L, DN_HEAD_V), jnp.float32)
    w_out = nrm(ks[15], (L, D_MIX, D_MODEL), jnp.float32) * D_MIX ** -0.5
    final_norm_w = 1.0 + 0.01 * nrm(ks[16], (D_MODEL,), jnp.float32)
    return {"x": x, "norm_w": norm_w, "w_in": w_in, "lru_conv_w": lru_conv_w,
            "lru_conv_b": lru_conv_b, "lru_wa": lru_wa, "lru_ba": lru_ba, "lru_wx": lru_wx,
            "lru_bx": lru_bx, "lru_lambda": lru_lambda, "lru_norm_w": lru_norm_w,
            "dn_conv_w": dn_conv_w, "dn_A_log": dn_A_log, "dn_dt_bias": dn_dt_bias,
            "dn_norm_w": dn_norm_w, "w_out": w_out, "final_norm_w": final_norm_w}

def reference(x, norm_w, w_in, lru_conv_w, lru_conv_b, lru_wa, lru_ba, lru_wx, lru_bx,
              lru_lambda, lru_norm_w, dn_conv_w, dn_A_log, dn_dt_bias, dn_norm_w, w_out,
              final_norm_w):
    h = x
    for l in range(DEPTH):
        h = hybrid_layer(h, norm_w[l], w_in[l], lru_conv_w[l], lru_conv_b[l], lru_wa[l], lru_ba[l],
                         lru_wx[l], lru_bx[l], lru_lambda[l], lru_norm_w[l], dn_conv_w[l],
                         dn_A_log[l], dn_dt_bias[l], dn_norm_w[l], w_out[l])
    return rmsnorm(h, final_norm_w)


_drawn_inputs = setup_inputs


def setup_inputs(seed=0):
    import zlib

    import numpy as np

    out = dict(_drawn_inputs(seed))
    spreads = {}
    factors = {'norm_w': 18.871,
     'lru_ba': 64.0,
     'lru_bx': 61.613,
     'lru_norm_w': 200.0,
     'dn_norm_w': 200.0,
     'final_norm_w': 184.742,
     'lru_conv_b': 26.392}
    for name, (base, spread) in spreads.items():
        noise = np.random.default_rng([zlib.crc32(name.encode()), seed]).standard_normal(out[name].shape)
        drawn = base * np.exp(spread * noise) if base else spread * noise
        out[name] = __import__('jax').numpy.asarray(drawn.astype(out[name].dtype))
    for name, factor in factors.items():
        out[name] = (out[name] * factor).astype(out[name].dtype)
    return out
```

```python
from contextlib import ExitStack

import concourse.bass as bass
from concourse import mybir

ALU = mybir.AluOpType
ACT = mybir.ActivationFunctionType
F32 = mybir.dt.float32
F32R = mybir.dt.float32r

P = 128
S = 1024
D = 1024
KT = D // P
C = 128
NC = S // C
NH = 8
HALF = 512
TAPS = 4
EPS = 1e-6
LRU_C = 8.0
QKVZ = 4
PASSES = 3
PIECE = 4
BLOCK_PIECES = 2 * KT * PASSES // PIECE
LEVELS = [2, 4, 8, 16, 32, 64]
COL_DN = 2 * D
COL_AB = COL_DN + QKVZ * D
SERIES = 8

NORM_W = 0
LRU_TAP = NORM_W + KT
LRU_B = LRU_TAP + TAPS * NH
LRU_BA = LRU_B + NH
LRU_BX = LRU_BA + NH
LRU_LAM = LRU_BX + NH
LRU_NW = LRU_LAM + NH
DN_NW = LRU_NW + NH
ROWS_A = DN_NW + 1
DN_TAP = P
ROWS_B = TAPS * 3 * NH

CHAIN = ("read", "solve", "update")
STATS_CHUNK = 5
STEPS = (
    [("scores", 0, 4), ("turn", 0, 4), ("first", 0, 2), ("out", 0, 4)]
    + [("level", k, 1) for k in range(len(LEVELS))]
    + [(name, c, f) for c in range(STATS_CHUNK) for name, f in zip(CHAIN, (1, 1, 2 if c < 4 else 1))]
    + [("read", STATS_CHUNK, 1), ("stats", 0, 0), ("solve", STATS_CHUNK, 1), ("update", STATS_CHUNK, 1)]
    + [(name, c, 1) for c in range(STATS_CHUNK + 1, NC) for name in CHAIN]
    + [("tail", 0, 0)]
)


def done_at(blocks):
    ends, pieces, j = [], 0, 0
    for n, (_, _, fill) in enumerate(STEPS):
        pieces += fill * blocks // QKVZ if blocks == QKVZ else fill
        ends.append([])
        while j < blocks and (pieces >= (j + 1) * BLOCK_PIECES or n == len(STEPS) - 1):
            ends[-1].append(j)
            j += 1
    return ends


def build(nc, x, norm_w, w_in, lru_conv_w, lru_conv_b, lru_wa, lru_ba, lru_wx, lru_bx, lru_lambda,
          lru_norm_w, dn_conv_w, dn_A_log, dn_dt_bias, dn_norm_w, w_out, final_norm_w, out):
    gc_rows = nc.dram_tensor("gc_rows", [NH * NC, C], F32).ap()
    w_in_v = w_in[0].rearrange("(t p) e -> p t e", p=P)
    keep = ExitStack()
    with keep:
        def sb(name, shape, dt=F32, stack=keep):
            return stack.enter_context(nc.sbuf_tensor(name, shape, dt))

        def sem(name, stack=keep):
            return stack.enter_context(nc.semaphore(name))

        yT = sb("yT", [P, 2 * NH, S])
        hT_hi = sb("hT_hi", [P, KT, S], F32R)
        hT_lo = sb("hT_lo", [P, KT, S], F32R)
        with ExitStack() as mix:
            ident = sb("ident", [P, P], stack=mix)
            par = sb("par", [P, P + ROWS_B], stack=mix)
            beta = sb("beta", [P, NH, NC], stack=mix)
            gc = sb("gc", [P, NH, NC], stack=mix)
            egc = sb("egc", [P, NH, NC], stack=mix)
            negegc = sb("negegc", [P, NH, NC], stack=mix)
            eglast = sb("eglast", [P, NH, NC], stack=mix)
            ekd = sb("ekd", [P, NH, NC], stack=mix)
            sp8 = sb("sp8", [P, 2, NH], stack=mix)
            triu = sb("triu", [P, P], stack=mix)
            masks = sb("masks", [P, 1 + len(LEVELS), P], stack=mix)

            first_block(nc, locals())
            mixer_block(nc, locals())
        with ExitStack() as last:
            output_block(nc, locals(), last)


def first_block(nc, env):
    (x, w_in_v, gc_rows, ident, par, beta, gc, egc, negegc, eglast, ekd, sp8, triu, masks, hT_hi, hT_lo) = (
        env[k] for k in "x w_in_v gc_rows ident par beta gc egc negegc eglast ekd sp8 triu masks hT_hi hT_lo".split())
    GATES = NH * NC
    GATE_STEPS = 15 + SERIES
    with ExitStack() as st:
        def sb(name, shape, dt=F32):
            return st.enter_context(nc.sbuf_tensor(name, shape, dt))

        def ps(name, shape):
            return st.enter_context(nc.psum_tensor(name, shape, F32))

        def sem(name):
            return st.enter_context(nc.semaphore(name))

        NX = 3
        xs = sb("xs", [P, NX, D])
        junk = sb("junk", [P, D])
        h32 = sb("h32", [P, 2, KT, P])
        rowsA = sb("rowsA", [ROWS_A, P])
        rowsB = sb("rowsB", [ROWS_B, P])
        ones = sb("ones", [P, P])
        rms = sb("rms", [P, 3, NC])
        wab = sb("wab", [P, KT, 2 * NH])
        wab_hi = sb("wab_hi", [P, KT, 2 * NH], F32R)
        wab_lo = sb("wab_lo", [P, KT, 2 * NH], F32R)
        alog = sb("alog", [P, 2, NH])
        aexp = sb("aexp", [P, NH])
        xcat = sb("xcat", [P, GATES + NH])
        sp = sb("sp", [P, 8, GATES + NH])
        g = sb("g", [P, NH, NC])
        gcrow_sb = sb("gcrow_sb", [GATES, C])
        tr = [ps(f"tr{i}", [P, 2, HALF]) for i in range(2)]
        pab = ps("pab", [P, NC, 2 * NH])
        ppar = ps("ppar", [P, HALF])
        pgc = ps("pgc", [P, HALF])
        pgl = ps("pgl", [P, HALF])

        x_loaded = [sem(f"x_loaded{i}") for i in range(NX)]
        rows_loaded = sem("rows_loaded")
        wab_loaded = sem("wab_loaded")
        alog_loaded = sem("alog_loaded")
        const = sem("const")
        squared = sem("squared")
        mean_done = sem("mean_done")
        root_done = sem("root_done")
        rms_done = sem("rms_done")
        x_scaled = sem("x_scaled")
        turned = sem("turned")
        h_ready = sem("h_ready")
        hi_ready = sem("hi_ready")
        lo_ready = sem("lo_ready")
        par_turned = sem("par_turned")
        par_ready = sem("par_ready")
        wab_split = sem("wab_split")
        ab_done = sem("ab_done")
        gate_act = sem("gate_act")
        gate_dve = sem("gate_dve")
        gate_pe = sem("gate_pe")
        rows_stored = sem("rows_stored")
        xt = x[0].rearrange("(n p) d -> n p d", p=P)

        with nc.Block() as block:
            @block.sync
            def _(sp_eng):
                for t in range(NX):
                    sp_eng.dma_start(xs[:, t, :], xt[t]).then_inc(x_loaded[t], 16)
                n = 0
                for name, rows in (("norm_w", KT), ("lru_conv_w", TAPS * NH), ("lru_conv_b", NH), ("lru_ba", NH),
                                   ("lru_bx", NH), ("lru_lambda", NH), ("lru_norm_w", NH), ("dn_norm_w", 1)):
                    src = env[name]
                    src = src.rearrange("o k (b p) -> (o k b) p", p=P) if len(src.shape) == 3 else \
                        src.rearrange("o (b p) -> (o b) p", p=P)
                    sp_eng.dma_start(rowsA[n:n + rows, :], src).then_inc(rows_loaded, 16)
                    n += rows
                sp_eng.dma_start(rowsB[:], env["dn_conv_w"].rearrange("o k (b p) -> (o k b) p", p=P)) \
                    .then_inc(rows_loaded, 16)
                sp_eng.dma_start(wab[:], w_in_v[:, :, COL_AB:COL_AB + 2 * NH]).then_inc(wab_loaded, 16)
                sp_eng.dma_start(alog[:, 0, :], env["dn_A_log"].to_broadcast([P, NH])).then_inc(alog_loaded, 16)
                sp_eng.dma_start(alog[:, 1, :], env["dn_dt_bias"].to_broadcast([P, NH])).then_inc(alog_loaded, 16)
                for t in range(NX, NC):
                    sp_eng.wait_ge(turned, t - NX + 1)
                    sp_eng.dma_start(xs[:, t % NX, :], xt[t]).then_inc(x_loaded[t % NX], 16)
                sp_eng.wait_ge(gate_act, 6)
                sp_eng.dma_start(gc_rows, gcrow_sb[:]).then_inc(rows_stored, 16)
                sp_eng.wait_ge(rows_stored, 16)

            @block.gpsimd
            def _(pool):
                nc.gpsimd.memset(ident[:], 0.0)
                nc.gpsimd.memset(ones[:], 1.0).then_inc(const, 1)
                pool.wait_ge(const, 1)
                nc.gpsimd.affine_select(out=ident[:], in_=ident[:], compare_op=ALU.not_equal, fill=1.0, base=0,
                                        pattern=[[-1, P]], channel_multiplier=1)
                nc.gpsimd.affine_select(out=triu[:], in_=ones[:], compare_op=ALU.is_ge, fill=0.0, base=0,
                                        pattern=[[1, P]], channel_multiplier=-1)
                nc.gpsimd.memset(masks[:], -1.0).then_inc(const, 1)
                pool.wait_ge(const, 2)
                n = 2
                for lv, b in enumerate([1] + LEVELS):
                    m = masks[:, lv, :].rearrange("p (n s b) -> p n s b", s=2, b=b)
                    for base, mult, step, fill_s in ((0, 1, -2 * b, None), (b - 1, -1, 2 * b, None)):
                        nc.gpsimd.affine_select(out=m, in_=m, compare_op=ALU.is_ge, fill=0.0, base=base,
                                                pattern=[[step, P // (2 * b)], [0, 2], [0, b]],
                                                channel_multiplier=mult).then_inc(const, 1)
                        n += 1
                        pool.wait_ge(const, n)
                    nc.gpsimd.memset(m[:, :, 0, :], 0.0).then_inc(const, 1)
                    n += 1
                    pool.wait_ge(const, n)
                pool.wait_ge(wab_split, 1)
                nc.gpsimd.tensor_tensor(wab_lo[:], wab[:], wab_hi[:].bitcast(F32), ALU.subtract).then_inc(wab_split, 1)
                for t in range(NC):
                    pool.wait_ge(hi_ready, t + 1)
                    nc.gpsimd.tensor_tensor(hT_lo[:, :, t * P:(t + 1) * P], h32[:, t % 2],
                                            hT_hi[:, :, t * P:(t + 1) * P].bitcast(F32),
                                            ALU.subtract).then_inc(lo_ready, 1)

            @block.scalar
            def _(act):
                for t in range(NC):
                    act.wait_ge(x_loaded[t % NX], 16 * (t // NX + 1))
                    nc.scalar.activation(junk[:], xs[:, t % NX, :], ACT.Square,
                                         accum_out=rms[:, 0, t:t + 1]).then_inc(squared, 1)
                    act.wait_ge(mean_done, t + 1)
                    nc.scalar.activation(rms[:, 1, t:t + 1], rms[:, 0, t:t + 1], ACT.Sqrt).then_inc(root_done, 1)
                    if t == 0:
                        act.wait_ge(wab_loaded, 16)
                        nc.scalar.activation(wab_hi[:], wab[:], ACT.Copy).then_inc(wab_split, 1)
                    if t >= 1:
                        act.wait_ge(h_ready, 2 * t)
                        nc.scalar.activation(hT_hi[:, :, (t - 1) * P:t * P], h32[:, (t - 1) % 2],
                                             ACT.Copy).then_inc(hi_ready, 1)
                act.wait_ge(h_ready, 2 * NC)
                nc.scalar.activation(hT_hi[:, :, (NC - 1) * P:], h32[:, (NC - 1) % 2], ACT.Copy).then_inc(hi_ready, 1)
                act.wait_ge(gate_dve, 2)
                nc.scalar.activation(sp[:, 0, :], xcat[:], ACT.Abs).then_inc(gate_act, 1)
                act.wait_ge(gate_act, 1)
                nc.scalar.activation(sp[:, 1, :], sp[:, 0, :], ACT.Exp, scale=-1.0).then_inc(gate_act, 1)
                act.wait_ge(alog_loaded, 32)
                nc.scalar.activation(aexp[:], alog[:, 0, :], ACT.Exp).then_inc(gate_act, 1)
                nc.scalar.activation(beta[:].rearrange("p h c -> p c h"), pab[:, :, 0:NH], ACT.Sigmoid) \
                    .then_inc(gate_act, 1)
                act.wait_ge(gate_pe, 2)
                nc.scalar.activation(egc[:], pgc[:, 0:GATES].rearrange("p (h c) -> p h c", h=NH), ACT.Exp) \
                    .then_inc(gate_act, 1)
                nc.scalar.activation(gcrow_sb[:], pgc[0:GATES, P:2 * P], ACT.Copy).then_inc(gate_act, 1)
                act.wait_ge(gate_pe, 3)
                nc.scalar.activation(eglast[:], pgl[:, 0:GATES].rearrange("p (h c) -> p h c", h=NH), ACT.Exp) \
                    .then_inc(gate_act, 1)
                act.wait_ge(gate_dve, GATE_STEPS)
                nc.scalar.activation(ekd[:], ekd[:], ACT.Exp).then_inc(gate_act, 1)

            @block.vector
            def _(dve):
                def evacuate(t):
                    for f in range(2):
                        dve.wait_ge(turned, t + 1)
                        if f == 0 and t >= 2:
                            dve.wait_ge(lo_ready, t - 1)
                        nc.vector.tensor_tensor(
                            h32[:, t % 2, 4 * f:4 * f + 4, :], tr[t % 2][:, f, :].rearrange("p (d s) -> p d s", s=P),
                            par[:, NORM_W + 4 * f:NORM_W + 4 * f + 4].unsqueeze(2).to_broadcast([P, 4, P]),
                            ALU.mult).then_inc(h_ready, 1)

                for t in range(NC):
                    dve.wait_ge(squared, t + 1)
                    nc.vector.tensor_scalar(rms[:, 0, t:t + 1], rms[:, 0, t:t + 1], 1.0 / D, EPS, ALU.mult,
                                            ALU.add).then_inc(mean_done, 1)
                    dve.wait_ge(root_done, t + 1)
                    nc.vector.reciprocal(rms[:, 2, t:t + 1], rms[:, 1, t:t + 1]).then_inc(rms_done, 1)
                    dve.wait_ge(rms_done, t + 1)
                    nc.vector.tensor_scalar(xs[:, t % NX, :], xs[:, t % NX, :], rms[:, 2, t:t + 1], None,
                                            ALU.mult).then_inc(x_scaled, 1)
                    if t == 0:
                        dve.wait_ge(par_turned, 1)
                        nc.vector.tensor_copy(par[:, 0:ROWS_A], ppar[:, 0:ROWS_A])
                        nc.vector.tensor_copy(par[:, DN_TAP:], ppar[:, DN_TAP:DN_TAP + ROWS_B]).then_inc(par_ready, 1)
                        dve.wait_ge(par_ready, 1)
                    if t >= 1:
                        evacuate(t - 1)
                evacuate(NC - 1)
                nc.vector.tensor_scalar(xcat[:, GATES:], par[:, LRU_LAM:LRU_LAM + NH], -1.0, None, ALU.mult) \
                    .then_inc(gate_dve, 1)
                dve.wait_ge(ab_done, NC)
                dve.wait_ge(alog_loaded, 32)
                nc.vector.tensor_tensor(xcat[:, 0:GATES].rearrange("p (h c) -> p c h", h=NH), pab[:, :, NH:2 * NH],
                                        alog[:, 1, :].unsqueeze(1).to_broadcast([P, NC, NH]), ALU.add) \
                    .then_inc(gate_dve, 1)
                count = [2]

                def step(ins):
                    count[0] += 1
                    ins.then_inc(gate_dve, 1)
                    dve.wait_ge(gate_dve, count[0])

                z, den, s1, s2, acc = (sp[:, k, :] for k in (1, 2, 3, 4, 5))
                dve.wait_ge(gate_act, 2)
                step(nc.vector.tensor_scalar(den, z, 2.0, None, ALU.add))
                step(nc.vector.reciprocal(den, den))
                step(nc.vector.tensor_tensor(s1, z, den, ALU.mult))
                step(nc.vector.tensor_tensor(s2, s1, s1, ALU.mult))
                step(nc.vector.tensor_scalar(acc, s2, 1.0 / (2 * SERIES + 1), None, ALU.mult))
                for k in range(SERIES - 1, 0, -1):
                    step(nc.vector.scalar_tensor_tensor(out=acc, in0=acc, scalar=1.0 / (2 * k + 1), in1=s2,
                                                        op0=ALU.add, op1=ALU.mult))
                step(nc.vector.scalar_tensor_tensor(out=acc, in0=acc, scalar=1.0, in1=s1, op0=ALU.add, op1=ALU.mult))
                step(nc.vector.tensor_scalar(s2, xcat[:], 0.0, None, ALU.max))
                step(nc.vector.scalar_tensor_tensor(out=acc, in0=acc, scalar=2.0, in1=s2, op0=ALU.mult, op1=ALU.add))
                step(nc.vector.tensor_scalar(sp8[:, 0, :], acc[:, GATES:], LRU_C, None, ALU.mult))
                step(nc.vector.tensor_scalar(sp8[:, 1, :], acc[:, GATES:], -LRU_C, None, ALU.mult))
                dve.wait_ge(gate_act, 3)
                step(nc.vector.scalar_tensor_tensor(
                    out=g[:], in0=acc[:, 0:GATES].rearrange("p (h c) -> p h c", h=NH), scalar=-1.0,
                    in1=aexp[:].unsqueeze(2).to_broadcast([P, NH, NC]), op0=ALU.mult, op1=ALU.mult))
                dve.wait_ge(gate_pe, 3)
                dve.wait_ge(gate_act, 7)
                step(nc.vector.tensor_copy(gc[:], pgc[:, 0:GATES].rearrange("p (h c) -> p h c", h=NH)))
                step(nc.vector.tensor_scalar(negegc[:], egc[:], -1.0, None, ALU.mult))
                step(nc.vector.tensor_tensor(ekd[:], pgl[:, 0:GATES].rearrange("p (h c) -> p h c", h=NH), gc[:],
                                             ALU.subtract))
                assert count[0] == GATE_STEPS

            @block.tensor
            def _(pe):
                pe.wait_ge(const, 2)
                pe.wait_ge(rows_loaded, 16 * 9)
                nc.tensor.transpose(ppar[:, 0:ROWS_A], rowsA[:], ident[0:ROWS_A, 0:ROWS_A])
                nc.tensor.transpose(ppar[:, P:P + ROWS_B], rowsB[:], ident[0:ROWS_B, 0:ROWS_B]).then_inc(par_turned, 1)

                def gates(t):
                    pe.wait_ge(lo_ready, t + 1)
                    for n, (a, b) in enumerate(((hT_hi, wab_hi), (hT_hi, wab_lo), (hT_lo, wab_hi))):
                        for d in range(KT):
                            last = nc.tensor.matmul(pab[:, t, :], a[:, d, t * P:(t + 1) * P], b[:, d, :],
                                                    start=(t == 0 and n == 0 and d == 0),
                                                    stop=(n == 2 and d == KT - 1), skip_group_check=True)
                    last.then_inc(ab_done, 1)

                for t in range(NC):
                    pe.wait_ge(x_scaled, t + 1)
                    if t >= 2:
                        pe.wait_ge(h_ready, 2 * (t - 1))
                    for d in range(KT):
                        last = nc.tensor.transpose(tr[t % 2][:, d // 4, (d % 4) * P:(d % 4 + 1) * P],
                                                   xs[:, t % NX, d * P:(d + 1) * P], ident[:])
                    last.then_inc(turned, 1)
                    if t == 2:
                        pe.wait_ge(wab_split, 2)
                    if t >= 2:
                        gates(t - 2)
                gates(NC - 2)
                gates(NC - 1)
                pe.wait_ge(gate_dve, GATE_STEPS - 3)
                gf = g[:].rearrange("p h c -> p (h c)")
                nc.tensor.matmul(pgc[:, 0:GATES], triu[:], gf, start=True, stop=True).then_inc(gate_pe, 1)
                nc.tensor.matmul(pgc[0:GATES, P:2 * P], gf, triu[:], start=True, stop=True).then_inc(gate_pe, 1)
                nc.tensor.matmul(pgl[:, 0:GATES], ones[:], gf, start=True, stop=True).then_inc(gate_pe, 1)


def mixer_block(nc, env):
    (w_in_v, gc_rows, yT, ident, par, beta, gc, egc, negegc, eglast, ekd, sp8, triu, masks, hT_hi, hT_lo) = (
        env[k] for k in
        "w_in_v gc_rows yT ident par beta gc egc negegc eglast ekd sp8 triu masks hT_hi hT_lo".split())
    NL = len(LEVELS)
    HC = C // 2
    DN_BLOCKS = QKVZ * NH
    DN_CONVS = 3 * NH
    X_UPS = 4 * (NL - 1) + 2
    with ExitStack() as st:
        def sb(name, shape, dt=F32):
            return st.enter_context(nc.sbuf_tensor(name, shape, dt))

        def ps(name, shape):
            return st.enter_context(nc.psum_tensor(name, shape, F32))

        def sem(name):
            return st.enter_context(nc.semaphore(name))

        w_raw = [sb(f"w_raw{i}", [P, KT, P]) for i in range(2)]
        w_hi = [sb(f"w_hi{i}", [P, KT, P], F32R) for i in range(2)]
        w_lo = [sb(f"w_lo{i}", [P, KT, P], F32R) for i in range(2)]
        qkv = [[sb(f"{n}T{i}", [P, S]) for n in "qkv"] for i in range(2)]
        kd = sb("kd", [P, NC, P])
        vos = [sb(f"vo{i}", [P, NC, P]) for i in range(2)]
        ets = [sb(f"et{i}", [P, NC, P]) for i in range(2)]
        qe = sb("qe", [P, 2, NC])
        state = sb("state", [P, P])
        rhs = sb("rhs", [P, P])
        wsol = sb("wsol", [P, P])
        o1 = sb("o1", [P, P])
        junk = sb("junk2", [P, P])
        sse = sb("sse", [P, 2, NC])
        small = sb("small", [P, 8, NC])
        seed = sb("seed", [P, 2])
        wg = [sb(f"wg{i}", [P, 2, P]) for i in range(2)]
        gt = yT[:, 2, :].rearrange("p (c i) -> p c i", i=P)
        xx = [yT[:, 3, HALF * b:HALF * (b + 1)].rearrange("p (c i) -> p c i", i=P) for b in range(2)]
        xt = [yT[:, 4, HALF * b:HALF * (b + 1)].rearrange("p (c i) -> p c i", i=P) for b in range(2)]
        zz = [yT[:, 5, HALF * b:HALF * (b + 1)].rearrange("p (c i) -> p c i", i=P) for b in range(2)]
        lm = [[yT[:, 6 + k, HALF * b:HALF * (b + 1)].rearrange("p (c i) -> p c i", i=P) for b in range(2)]
              for k in range(2)]
        pp = [ps(f"pp{i}", [P, S]) for i in range(2)]
        bank = [ps(f"bank{i}", [P, HALF]) for i in range(4)]

        w_loaded = [sem(f"w_loaded{i}") for i in range(2)]
        hi_split = sem("hi_split")
        lo_split = sem("lo_split")
        projected = sem("projected")
        tap_first = sem("tap_first")
        tapped = sem("tapped")
        gated = sem("gated")
        rows_in = sem("rows_in")
        sq_done = sem("sq_done")
        stats_done = sem("stats_done")
        stat_step = sem("stat_step")
        root_n = sem("root_n")
        turned = sem("turned2")
        kv_ready = sem("kv_ready")
        v_ready = sem("v_ready")
        scored = sem("scored")
        gap_done = sem("gap_done")
        decay_exp = sem("decay_exp")
        et_done = sem("et_done")
        gt_done = sem("gt_done")
        attn_ready = sem("attn_ready")
        lm_done = sem("lm_done")
        xt_first = sem("xt_first")
        x_turned = sem("x_turned")
        x_first = sem("x_first")
        z_done = sem("z_done")
        z_ready = sem("z_ready")
        x_done = sem("x_done")
        x_up = sem("x_up")
        read_done = sem("read_done")
        rhs_ready = sem("rhs_ready")
        o1_ready = sem("o1_ready")
        solved = sem("solved")
        w_ready = sem("w_ready")
        state_sum = sem("state_sum")
        attn_done = sem("attn_done")
        state_ready = sem("state_ready")
        o_ready = sem("o_ready")
        o_squared = sem("o_squared")
        o_mean = sem("o_mean")
        o_root = sem("o_root")
        o_rec = sem("o_rec")
        o_scaled = sem("o_scaled")
        o_turned = sem("o_turned")
        y_done = sem("y_done")
        wg_loaded = [sem(f"wg_loaded{i}") for i in range(2)]
        lgate_done = sem("lgate_done")
        lru_act = sem("lru_act")
        lru_ix = sem("lru_ix")
        lru_dve = sem("lru_dve")
        lru_h = sem("lru_h")
        lstat_done = sem("lstat_done")
        lcast_done = sem("lcast_done")
        LA, LD = 8, 6

        DN_DONE = done_at(QKVZ)
        LRU_DONE = done_at(2)

        def column(j, h):
            return COL_DN + j * D + h * P

        def banks_of(level):
            p, q, r, s = 0, 1, 2, 3
            for _ in range(level):
                p, q, r, s = r, p, s, q
            return p, q, (r, s), (p, q)

        with nc.Block() as block:
            @block.sync
            def _(sp):
                def load(j, count, col, n):
                    sp.wait_ge(lo_split, n - 1)
                    sp.dma_start(w_raw[j % 2][:], w_in_v[:, :, bass.ds(col, P)]).then_inc(w_loaded[j % 2], 16)

                def head(h):
                    for j in range(QKVZ):
                        load(j, 0, column(j, h), QKVZ * h + j)

                for j in range(QKVZ):
                    if j < 2:
                        sp.dma_start(w_raw[j][:], w_in_v[:, :, column(j, 0):column(j, 0) + P]) \
                            .then_inc(w_loaded[j], 16)
                    else:
                        load(j, 0, column(j, 0), j)
                with sp.Fori(1, NH) as h:
                    head(h)

                def gate_weights(l, b):
                    sp.dma_start(wg[b][:, 0, :], env["lru_wa"][0, bass.ds(l, 1)].rearrange("o i j -> i (o j)")) \
                        .then_inc(wg_loaded[b], 16)
                    sp.dma_start(wg[b][:, 1, :], env["lru_wx"][0, bass.ds(l, 1)].rearrange("o i j -> i (o j)")) \
                        .then_inc(wg_loaded[b], 16)

                def lru_head(l, b):
                    load(0, 0, l * P, DN_BLOCKS + 2 * l)
                    load(1, 0, D + l * P, DN_BLOCKS + 2 * l + 1)
                    if isinstance(l, int) and l < 2:
                        gate_weights(l, b)
                    else:
                        sp.wait_ge(lgate_done, 2 * (l - 1))
                        gate_weights(l, b)

                lru_head(0, 0)
                lru_head(1, 1)
                with sp.Fori(1, NH // 2) as p:
                    lru_head(2 * p, 0)
                    lru_head(2 * p + 1, 1)

            @block.gpsimd
            def _(pool):
                def split(j, n):
                    pool.wait_ge(hi_split, n + 1)
                    nc.gpsimd.tensor_tensor(w_lo[j % 2][:], w_raw[j % 2][:], w_hi[j % 2][:].bitcast(F32),
                                            ALU.subtract).then_inc(lo_split, 1)

                def prepare(h, b):
                    q, kk, _ = qkv[b]
                    pool.wait_ge(gated, QKVZ * h + 2)
                    if not (isinstance(h, int) and h == 0):
                        pool.wait_ge(x_done, 2 * NL * h)
                        pool.wait_ge(z_ready, 2 * NL * h)
                    nc.gpsimd.tensor_tensor(yT[:, 2, :], kk[:], kk[:], ALU.mult).then_inc(sq_done, 1)
                    nc.gpsimd.tensor_tensor(yT[:, 3, :], q[:], q[:], ALU.mult).then_inc(sq_done, 1)
                    pool.wait_ge(rows_in, 16 * (h + 1))
                    nc.gpsimd.tensor_tensor(ets[b][:], gc[:, bass.ds(h, 1), :].rearrange("p o c -> p (o c)")
                                            .unsqueeze(2).to_broadcast([P, NC, P]), ets[b][:],
                                            ALU.subtract).then_inc(gap_done, 1)

                def weigh(h, b):
                    pool.wait_ge(decay_exp, 2 * h + 2)
                    nc.gpsimd.tensor_tensor(ets[b][:], ets[b][:], triu[:].unsqueeze(1).to_broadcast([P, NC, P]),
                                            ALU.mult).then_inc(et_done, 1)
                    pool.wait_ge(stat_step, 5 * h + 3)
                    pool.wait_ge(et_done, 2 * h + 1)
                    nc.gpsimd.tensor_tensor(ets[b][:], ets[b][:], small[:, 2, :].unsqueeze(2)
                                            .to_broadcast([P, NC, P]), ALU.mult).then_inc(et_done, 1)

                def step(name, k, h, b):
                    if name == "scores":
                        masked(0, h)
                        masked(1, h)
                    if name == "level" and k + 2 <= NL:
                        masked(k + 2, h)
                    if name == "read" and k == 2 and not (isinstance(h, int) and h == NH - 1):
                        prepare(h + 1, 1 - b)
                    if name == "solve" and k == STATS_CHUNK and not (isinstance(h, int) and h == NH - 1):
                        weigh(h + 1, 1 - b)

                def masked(lv, h):
                    for a in range(2):
                        if lv == 0:
                            pool.wait_ge(gt_done, 2 * h + a + 1)
                        if lv == 2:
                            pool.wait_ge(xt_first, 2 * h + a + 1)
                        if lv >= 3:
                            pool.wait_ge(z_done, 2 * NL * h + 2 * (lv - 3) + a + 1)
                        nc.gpsimd.tensor_tensor(lm[lv % 2][a], gt[:, 4 * a:4 * a + 4, :],
                                                masks[:, lv, :].unsqueeze(1).to_broadcast([P, 4, P]),
                                                ALU.mult).then_inc(lm_done, 1)

                def slot(h, b, n0, ends):
                    for s, (name, k, _) in enumerate(STEPS):
                        step(name, k, h, b)
                        for j in ends[s]:
                            split(j, n0 + j + 2)

                split(0, 0)
                split(1, 1)
                for j in range(QKVZ - 1):
                    split(j, j + 2)
                prepare(0, 0)
                split(QKVZ - 1, QKVZ + 1)
                weigh(0, 0)
                slot(0, 0, QKVZ, DN_DONE)
                with pool.Fori(0, (NH - 2) // 2) as p:
                    slot(2 * p + 1, 1, QKVZ * (2 * p + 2), DN_DONE)
                    slot(2 * p + 2, 0, QKVZ * (2 * p + 3), DN_DONE)
                slot(NH - 1, 1, DN_BLOCKS, LRU_DONE)

                def lru(l, b, more=True):
                    mix(l - 1, 1 - b)
                    for j in range(2):
                        if more:
                            split(j, DN_BLOCKS + 2 * l + j + 2)

                def mix(l, b):
                    pool.wait_ge(lru_act, LA * l + 2)
                    nc.gpsimd.tensor_tensor(qkv[b][2][:], qkv[b][2][:], qkv[b][0][:], ALU.mult).then_inc(lru_ix, 1)

                with pool.Fori(0, (NH - 2) // 2) as p:
                    lru(2 * p + 1, 1)
                    lru(2 * p + 2, 0)
                lru(NH - 1, 1, False)
                mix(NH - 1, 1)

            @block.scalar
            def _(act):
                def split(j, n, count, used):
                    act.wait_ge(w_loaded[j % 2], count)
                    if used:
                        act.wait_ge(projected, n - 1)
                        act.wait_ge(lo_split, n - 1)
                    nc.scalar.activation(w_hi[j % 2][:], w_raw[j % 2][:], ACT.Copy).then_inc(hi_split, 1)

                def first_tap(j, h, b):
                    act.wait_ge(projected, QKVZ * h + j + 1)
                    col = DN_TAP + (TAPS - 1) * 3 * NH + j * NH
                    nc.scalar.activation(qkv[b][j][:], pp[j % 2][:], ACT.Copy,
                                         scale=par[:, bass.ds(col + h, 1)]).then_inc(tap_first, 1)

                def silu(j, h, b):
                    act.wait_ge(tapped, 3 * (3 * h + j + 1))
                    nc.scalar.activation(qkv[b][j][:], qkv[b][j][:], ACT.Silu).then_inc(gated, 1)

                def silu_z(h):
                    act.wait_ge(projected, QKVZ * h + QKVZ)
                    nc.scalar.activation(yT[:, bass.ds(NH + h, 1), :], pp[1][:].rearrange("p (o s) -> p o s", o=1),
                                         ACT.Silu).then_inc(gated, 1)

                def ended(j, h, b, last=False):
                    n = QKVZ * h + j
                    if j < 2:
                        split(j, n + 2, 16 * (2 * h + 2), True)
                    else:
                        split(j, n + 2, 16 * (2 * h + 3), True)
                    if j < 3:
                        first_tap(j, h, b)
                    else:
                        silu_z(h)

                def lru_split(l, j):
                    split(j, DN_BLOCKS + 2 * l + j, 16 * (DN_BLOCKS // 2 + l + 1), True)

                def lru_tap(l, b):
                    act.wait_ge(projected, DN_BLOCKS + 2 * l + 1)
                    nc.scalar.activation(qkv[b][0][:], pp[0][:], ACT.Identity,
                                         scale=par[:, bass.ds(LRU_TAP + (TAPS - 1) * NH + l, 1)],
                                         bias=par[:, bass.ds(LRU_B + l, 1)]).then_inc(tap_first, 1)

                def lru_silu(l):
                    act.wait_ge(projected, DN_BLOCKS + 2 * l + 2)
                    nc.scalar.activation(yT[:, bass.ds(l, 1), :], pp[1][:].rearrange("p (o s) -> p o s", o=1),
                                         ACT.Silu).then_inc(gated, 1)

                def rows(h, b):
                    act.dma_start(ets[b][:].rearrange("p c i -> p (c i)"),
                                  gc_rows.rearrange("(h c) i -> h (c i)", h=NH)[bass.ds(h, 1), :]
                                  .to_broadcast([P, S])).then_inc(rows_in, 16)

                def decay(h, b):
                    act.wait_ge(gap_done, h + 1)
                    nc.scalar.activation(ets[b][:], ets[b][:], ACT.Relu).then_inc(decay_exp, 1)
                    act.wait_ge(decay_exp, 2 * h + 1)
                    nc.scalar.activation(ets[b][:], ets[b][:], ACT.Exp, scale=-1.0).then_inc(decay_exp, 1)

                def key_norm(h):
                    act.wait_ge(stat_step, 5 * h + 1)
                    nc.scalar.activation(small[:, 0, :], sse[:, 0, :], ACT.Sqrt).then_inc(root_n, 1)

                def out_root(h):
                    act.wait_ge(o_mean, h + 1)
                    nc.scalar.activation(small[:, 5, :], small[:, 5, :], ACT.Sqrt).then_inc(o_root, 1)

                def step(name, k, h, b, last):
                    first = isinstance(h, int) and h == 0
                    if name == "scores" and not first:
                        out_root(h - 1)
                    if name == "scores" and not last:
                        rows(h + 1, 1 - b)
                    if name == "turn":
                        for a in range(2):
                            act.wait_ge(turned, 4 * h + a + 1)
                            for c in range(4):
                                t = 4 * a + c
                                last_copy = nc.scalar.activation(kd[:, t, :], bank[a][:, c * P:(c + 1) * P],
                                                                 ACT.Copy, scale=small[:, 3, t:t + 1])
                            last_copy.then_inc(kv_ready, 1)
                    if name == "first":
                        for a in range(2):
                            act.wait_ge(x_turned, 2 * h + a + 1)
                            nc.scalar.activation(xx[a], bank[2 + a][:].rearrange("p (c i) -> p c i", i=P),
                                                 ACT.Copy).then_inc(x_first, 1)
                    if name == "read" and k == 3 and not last:
                        decay(h + 1, 1 - b)
                    if name == "solve" and k == STATS_CHUNK and not last:
                        key_norm(h + 1)
                    if name == "level":
                        zb = banks_of(k)[0:2]
                        rows_, cols = (slice(HC, P), slice(0, HC)) if k == NL - 1 else (slice(0, P), slice(0, P))
                        for a in range(2):
                            act.wait_ge(z_done, 2 * NL * h + 2 * k + a + 1)
                            nc.scalar.activation(zz[a][rows_, :, cols],
                                                 bank[zb[a]][:].rearrange("p (c i) -> p c i", i=P)[rows_, :, cols],
                                                 ACT.Copy).then_inc(z_ready, 1)
                    if name == "solve":
                        act.wait_ge(solved, NC * h + k + 1)
                        nc.scalar.activation(wsol[:], bank[2][:, 0:P], ACT.Copy).then_inc(w_ready, 1)
                        if k > 0:
                            act.wait_ge(read_done, 2 * ((NC - 1) * h + k))
                            nc.scalar.activation(o1[:], bank[1][:, 0:P], ACT.Copy,
                                                 scale=egc[:, bass.ds(h, 1), k]).then_inc(o1_ready, 1)
                    if name == "update":
                        if k > 0:
                            square(k - 1, h, b)
                    if name == "tail":
                        square(NC - 1, h, b)

                def square(c, h, b):
                    act.wait_ge(o_ready, NC * h + c + 1)
                    if c > 0:
                        act.wait_ge(o_squared, NC * h + c)
                    nc.scalar.activation(junk[:], vos[b][:, c, :], ACT.Square,
                                         accum_out=small[:, 4, c:c + 1]).then_inc(o_squared, 1)

                def slot(h, b, last=False):
                    later = []
                    for s, (name, k, _) in enumerate(STEPS):
                        step(name, k, h, b, last)
                        for j in DN_DONE[s]:
                            ended(j, h + 1, 1 - b)
                        for j in (DN_DONE[s - 3] if s >= 3 else []):
                            if j < 3:
                                silu(j, h + 1, 1 - b)

                rows(0, 0)
                split(0, 0, 16, False)
                split(1, 1, 16, False)
                for j in range(QKVZ):
                    ended(j, 0, 0)
                    if j < 3:
                        silu(j, 0, 0)
                decay(0, 0)
                key_norm(0)
                slot(0, 0)
                with act.Fori(0, (NH - 2) // 2) as p:
                    slot(2 * p + 1, 1)
                    slot(2 * p + 2, 0)
                for s, (name, k, _) in enumerate(STEPS):
                    step(name, k, NH - 1, 1, True)
                    for j in LRU_DONE[s]:
                        lru_split(1, j)
                        if j == 0:
                            lru_tap(0, 0)
                        else:
                            lru_silu(0)
                out_root(NH - 1)

                def elementwise(l, b):
                    _, r, i = qkv[b]
                    for k, (dst, col) in enumerate(((r, LRU_BA), (i, LRU_BX))):
                        act.wait_ge(lgate_done, 2 * l + k + 1)
                        for f in range(2):
                            last = nc.scalar.activation(dst[:, HALF * f:HALF * (f + 1)], bank[2 * k + f][:],
                                                        ACT.Sigmoid, bias=par[:, bass.ds(col + l, 1)])
                        last.then_inc(lru_act, 1)
                    act.wait_ge(lru_act, LA * l + 1)
                    act.wait_ge(lru_h, l + 1)
                    nc.scalar.activation(kd[:], r[:].rearrange("p (c i) -> p c i", i=P), ACT.Tanh,
                                         scale=sp8[:, 0, bass.ds(l, 1)]).then_inc(lru_act, 1)
                    nc.scalar.activation(vos[0][:], r[:].rearrange("p (c i) -> p c i", i=P), ACT.Exp,
                                         scale=sp8[:, 1, bass.ds(l, 1)]).then_inc(lru_act, 1)
                    act.wait_ge(lru_act, LA * l + 4)
                    nc.scalar.activation(r[:].rearrange("p (c i) -> p c i", i=P), vos[0][:], ACT.Square) \
                        .then_inc(lru_act, 1)
                    act.wait_ge(lru_dve, LD * l + 1)
                    nc.scalar.activation(kd[:], kd[:], ACT.Sqrt).then_inc(lru_act, 1)

                def h_square(l, b):
                    act.wait_ge(lru_h, l + 2)
                    nc.scalar.activation(qkv[b][1][:], qkv[b][0][:], ACT.Square).then_inc(lru_act, 1)

                def norm_root(l):
                    act.wait_ge(lru_dve, LD * l + 3)
                    nc.scalar.activation(small[:, 5, :], small[:, 5, :], ACT.Sqrt).then_inc(lru_act, 1)

                def lru(l, b, more=True):
                    elementwise(l - 1, 1 - b)
                    if more:
                        lru_split(l + 1, 0)
                    lru_tap(l, b)
                    h_square(l - 1, 1 - b)
                    norm_root(l - 1)
                    if more:
                        lru_split(l + 1, 1)
                    lru_silu(l)

                with act.Fori(0, (NH - 2) // 2) as p:
                    lru(2 * p + 1, 1)
                    lru(2 * p + 2, 0)
                lru(NH - 1, 1, False)
                elementwise(NH - 1, 1)
                h_square(NH - 1, 1)
                norm_root(NH - 1)

            @block.vector
            def _(dve):
                def tap(t, acc, src, col, count):
                    nc.vector.scalar_tensor_tensor(out=acc[:, t:], in0=src[:, 0:S - t], scalar=col, in1=acc[:, t:],
                                                   op0=ALU.mult, op1=ALU.add).then_inc(tapped, 1)

                def taps(t, j, h, b):
                    base = 3 * (3 * h + j)
                    if t == 1:
                        dve.wait_ge(tap_first, 3 * h + j + 1)
                    else:
                        dve.wait_ge(tapped, base + t - 1)
                    tap(t, qkv[b][j], pp[j % 2], par[:, bass.ds(DN_TAP + (TAPS - 1 - t) * 3 * NH + j * NH + h, 1)], 0)

                def lru_taps(l, b):
                    for t in range(1, TAPS):
                        if t == 1:
                            dve.wait_ge(tap_first, DN_CONVS + l + 1)
                        else:
                            dve.wait_ge(tapped, 3 * (DN_CONVS + l) + t - 1)
                        tap(t, qkv[b][0], pp[0], par[:, bass.ds(LRU_TAP + (TAPS - 1 - t) * NH + l, 1)], 0)

                def col(tile, h, c):
                    return tile[:, bass.ds(h, 1), c]

                def stats(h, b):
                    dve.wait_ge(stats_done, h + 1)
                    nc.vector.tensor_scalar(sse[:].rearrange("p a c -> p (a c)"), bank[3][:, 0:2 * NC], EPS, None,
                                            ALU.add).then_inc(stat_step, 1)
                    dve.wait_ge(stat_step, 5 * h + 1)
                    nc.vector.reciprocal(small[:, 1, :], sse[:, 0, :]).then_inc(stat_step, 1)
                    dve.wait_ge(stat_step, 5 * h + 2)
                    nc.vector.tensor_tensor(small[:, 2:3, :], small[:, 1:2, :], beta[:, bass.ds(h, 1), :],
                                            ALU.mult).then_inc(stat_step, 1)
                    dve.wait_ge(stat_step, 5 * h + 3)
                    nc.vector.tensor_tensor(small[:, 3:4, :], small[:, 2:3, :], ekd[:, bass.ds(h, 1), :],
                                            ALU.mult).then_inc(stat_step, 1)
                    nc.vector.tensor_scalar(qe[:, b, :], sse[:, 1, :], EPS * P, None, ALU.mult) \
                        .then_inc(stat_step, 1)

                def out_mean(h, b):
                    dve.wait_ge(o_squared, NC * (h + 1))
                    nc.vector.scalar_tensor_tensor(out=small[:, 5, :], in0=small[:, 4, :], scalar=1.0 / P,
                                                   in1=qe[:, b, :], op0=ALU.mult, op1=ALU.add).then_inc(o_mean, 1)

                def out_scale(h, b):
                    dve.wait_ge(o_root, h + 1)
                    nc.vector.reciprocal(small[:, 7, :], small[:, 5, :]).then_inc(o_rec, 1)
                    dve.wait_ge(o_rec, h + 1)
                    for a in range(2):
                        v = vos[b][:, 4 * a:4 * a + 4, :]
                        nc.vector.tensor_tensor(v, v, small[:, 7, 4 * a:4 * a + 4].unsqueeze(2)
                                                .to_broadcast([P, 4, P]), ALU.mult).then_inc(o_scaled, 1)

                def out_gate(h):
                    dve.wait_ge(gated, QKVZ * (h + 1))
                    for a in range(2):
                        dve.wait_ge(o_turned, 2 * h + a + 1)
                        y = yT[:, bass.ds(NH + h, 1), HALF * a:HALF * (a + 1)]
                        nc.vector.scalar_tensor_tensor(out=y, in0=bank[a][:].rearrange("p (o s) -> p o s", o=1),
                                                       scalar=par[:, DN_NW:DN_NW + 1], in1=y, op0=ALU.mult,
                                                       op1=ALU.mult).then_inc(y_done, 1)

                def step(name, k, h, b):
                    first = isinstance(h, int) and h == 0
                    et, vo = ets[b], vos[b]
                    if name == "scores":
                        if not first:
                            out_mean(h - 1, 1 - b)
                        dve.wait_ge(et_done, 2 * h + 2)
                        for a in range(2):
                            dve.wait_ge(scored, 4 * h + a + 1)
                            nc.vector.tensor_tensor(gt[:, 4 * a:4 * a + 4, :],
                                                    bank[a][:].rearrange("p (c i) -> p c i", i=P),
                                                    et[:, 4 * a:4 * a + 4, :], ALU.mult).then_inc(gt_done, 1)
                        for a in range(2):
                            dve.wait_ge(gt_done, 2 * h + a + 1)
                            dve.wait_ge(scored, 4 * h + a + 3)
                            nc.vector.tensor_tensor(et[:, 4 * a:4 * a + 4, :],
                                                    bank[2 + a][:].rearrange("p (c i) -> p c i", i=P),
                                                    et[:, 4 * a:4 * a + 4, :], ALU.mult).then_inc(attn_ready, 1)
                        for a in range(2):
                            dve.wait_ge(lm_done, 2 * (NL + 1) * h + a + 1)
                            nc.vector.tensor_tensor(xt[a], lm[0][a], ident[:].unsqueeze(1).to_broadcast([P, 4, P]),
                                                    ALU.add).then_inc(xt_first, 1)
                    if name == "turn":
                        dve.wait_ge(root_n, h + 1)
                        for a in range(2):
                            dve.wait_ge(turned, 4 * h + a + 3)
                            nc.vector.tensor_tensor(vo[:, 4 * a:4 * a + 4, :],
                                                    bank[2 + a][:].rearrange("p (c i) -> p c i", i=P),
                                                    small[:, 0, 4 * a:4 * a + 4].unsqueeze(2)
                                                    .to_broadcast([P, 4, P]), ALU.mult).then_inc(v_ready, 1)
                    if name == "turn" and not first:
                        out_scale(h - 1, 1 - b)
                    if name == "out" and not first:
                        out_gate(h - 1)
                    if name == "solve" and k == STATS_CHUNK and not (isinstance(h, int) and h == NH - 1):
                        stats(h + 1, 1 - b)
                    if name == "level":
                        xb = banks_of(k)[2:4]
                        for a in range(2):
                            for w, tile in enumerate((xx[a], xt[a])):
                                if k == NL - 1 and w == 0:
                                    continue
                                dve.wait_ge(x_done, 2 * NL * h + 2 * k + a + 1)
                                rows, cols = (slice(0, HC), slice(HC, P)) if k == NL - 1 else \
                                    (slice(0, P), slice(0, P))
                                tile = tile[rows, :, cols]
                                nc.vector.tensor_tensor(
                                    tile, bank[xb[a][w]][:].rearrange("p (c i) -> p c i", i=P)[rows, :, cols],
                                    tile, ALU.add).then_inc(x_up, 1)
                    if name == "read" and k > 0:
                        dve.wait_ge(read_done, 2 * ((NC - 1) * h + k - 1) + 1)
                        nc.vector.scalar_tensor_tensor(out=rhs[:], in0=bank[0][:, 0:P], scalar=col(negegc, h, k),
                                                       in1=vo[:, k, :], op0=ALU.mult, op1=ALU.add) \
                            .then_inc(rhs_ready, 1)
                    if name == "update":
                        if k < NC - 1:
                            dve.wait_ge(state_sum, (NC - 1) * h + k + 1)
                            if k == 0:
                                nc.vector.tensor_copy(state[:], bank[3][:, 0:P]).then_inc(state_ready, 1)
                            else:
                                dve.wait_ge(state_ready, (NC - 1) * h + k)
                                nc.vector.scalar_tensor_tensor(out=state[:], in0=state[:], scalar=col(eglast, h, k),
                                                               in1=bank[3][:, 0:P], op0=ALU.mult, op1=ALU.add) \
                                    .then_inc(state_ready, 1)
                        dve.wait_ge(attn_done, NC * h + k + 1)
                        if k == 0:
                            nc.vector.tensor_copy(vo[:, 0, :], bank[2][:, P:2 * P]).then_inc(o_ready, 1)
                        else:
                            dve.wait_ge(o1_ready, (NC - 1) * h + k)
                            nc.vector.tensor_tensor(vo[:, k, :], bank[2][:, P:2 * P], o1[:], ALU.add) \
                                .then_inc(o_ready, 1)
                def slot(h, b):
                    for s, (name, k, _) in enumerate(STEPS):
                        step(name, k, h, b)
                        for t in range(1, TAPS):
                            for j in (DN_DONE[s - t + 1] if s >= t - 1 else []):
                                if j < 3:
                                    taps(t, j, h + 1, 1 - b)

                nc.vector.memset(seed[:, 1:2], 0.0).then_inc(lru_h, 1)
                for j in range(3):
                    for t in range(1, TAPS):
                        taps(t, j, 0, 0)
                stats(0, 0)
                slot(0, 0)
                with dve.Fori(0, (NH - 2) // 2) as p:
                    slot(2 * p + 1, 1)
                    slot(2 * p + 2, 0)
                for s, (name, k, _) in enumerate(STEPS):
                    step(name, k, NH - 1, 1)
                    for j in LRU_DONE[s]:
                        if j == 0:
                            lru_taps(0, 0)
                out_mean(NH - 1, 1)
                out_scale(NH - 1, 1)
                out_gate(NH - 1)

                def elementwise(l, b):
                    xc, r, i = qkv[b]
                    kdf, vof = (t[:].rearrange("p c i -> p (c i)") for t in (kd, vos[0]))
                    dve.wait_ge(lru_act, LA * l + 5)
                    nc.vector.scalar_tensor_tensor(out=kdf, in0=r[:], scalar=1.0, in1=kdf, op0=ALU.add,
                                                   op1=ALU.mult).then_inc(lru_dve, 1)
                    dve.wait_ge(lru_act, LA * l + 6)
                    dve.wait_ge(lru_ix, l + 1)
                    nc.vector.tensor_tensor(i[:], i[:], kdf, ALU.mult).then_inc(lru_dve, 1)
                    dve.wait_ge(lru_dve, LD * l + 2)
                    nc.vector.tensor_tensor_scan(xc[:], vof, i[:], 0.0, ALU.mult, ALU.add).then_inc(lru_h, 1)

                def norm(l, b):
                    dve.wait_ge(lstat_done, l + 1)
                    nc.vector.tensor_scalar(small[:, 5, :], bank[0][:, 0:NC], 1.0 / P, EPS, ALU.mult, ALU.add) \
                        .then_inc(lru_dve, 1)
                    dve.wait_ge(lru_act, LA * l + 8)
                    nc.vector.reciprocal(small[:, 7, :], small[:, 5, :]).then_inc(lru_dve, 1)
                    y = yT[:, bass.ds(l, 1), :]
                    dve.wait_ge(gated, DN_BLOCKS + l + 1)
                    nc.vector.scalar_tensor_tensor(out=y, in0=qkv[b][0][:].rearrange("p (o s) -> p o s", o=1),
                                                   scalar=par[:, bass.ds(LRU_NW + l, 1)], in1=y, op0=ALU.mult,
                                                   op1=ALU.mult).then_inc(lru_dve, 1)
                    dve.wait_ge(lru_dve, LD * l + 5)
                    dve.wait_ge(lcast_done, l + 1)
                    for f in range(2):
                        yf = yT[:, bass.ds(l, 1), HALF * f:HALF * (f + 1)]
                        last = nc.vector.tensor_tensor(yf, bank[2 + f][:].rearrange("p (o s) -> p o s", o=1), yf,
                                                       ALU.mult)
                    last.then_inc(lru_dve, 1)

                def lru(l, b):
                    elementwise(l - 1, 1 - b)
                    lru_taps(l, b)
                    norm(l - 1, 1 - b)

                with dve.Fori(0, (NH - 2) // 2) as p:
                    lru(2 * p + 1, 1)
                    lru(2 * p + 2, 0)
                lru(NH - 1, 1)
                elementwise(NH - 1, 1)
                norm(NH - 1, 1)

            @block.tensor
            def _(pe):
                def pieces(first, count, n0, free):
                    for q in range(first, first + count):
                        j, m0 = q // BLOCK_PIECES, q % BLOCK_PIECES * PIECE
                        if m0 == 0:
                            pe.wait_ge(lo_split, n0 + j + 1)
                            free[j]()
                        for m in range(m0, m0 + PIECE):
                            f, r = m // (PASSES * KT), m % (PASSES * KT)
                            d, n = r // PASSES, r % PASSES
                            w, hh = ((w_hi, hT_hi), (w_hi, hT_lo), (w_lo, hT_hi))[n]
                            mm = nc.tensor.matmul(pp[j % 2][:, HALF * f:HALF * (f + 1)], w[j % 2][:, d, :],
                                                  hh[:, d, HALF * f:HALF * (f + 1)], start=(r == 0),
                                                  stop=(r == PASSES * KT - 1))
                            if m == 2 * PASSES * KT - 1:
                                mm.then_inc(projected, 1)

                def dn_free(h):
                    first = isinstance(h, int) and h == 0
                    return (
                        (lambda: None) if first else (lambda: pe.wait_ge(tapped, 9 * h)),
                        (lambda: None) if first else (lambda: pe.wait_ge(gated, QKVZ * h)),
                        lambda: pe.wait_ge(tapped, 9 * h + 3),
                        lambda: pe.wait_ge(tapped, 9 * h + 6),
                    )

                def lru_free(l):
                    return (lambda: pe.wait_ge(tapped, 3 * (DN_CONVS + l)),
                            lambda: pe.wait_ge(gated, DN_BLOCKS + l))

                def step(name, k, h, b):
                    first = isinstance(h, int) and h == 0
                    qT, kT, vT = qkv[b]
                    et, vo = ets[b], vos[b]

                    def tile(t, c):
                        return t[:, c * C:(c + 1) * C]

                    if name == "stats":
                        stats(h + 1)
                    if name == "scores":
                        if not first:
                            pe.wait_ge(o_ready, NC * h)
                        for a in range(4):
                            if a == 1 and not first:
                                pe.wait_ge(o1_ready, (NC - 1) * h)
                            if a == 3 and first:
                                pe.wait_ge(stat_step, 1)
                            for c in range(4):
                                t = 4 * (a % 2) + c
                                mm = nc.tensor.matmul(bank[a][:, c * P:(c + 1) * P], tile(kT, t),
                                                      tile(kT if a < 2 else qT, t), start=True, stop=True)
                            mm.then_inc(scored, 1)
                    if name == "turn":
                        for a in range(4):
                            if a < 2:
                                pe.wait_ge(gt_done, 2 * h + a + 1)
                            else:
                                pe.wait_ge(attn_ready, 2 * h + a - 1)
                            if a == 2:
                                pe.wait_ge(gated, QKVZ * h + 3)
                            for c in range(4):
                                mm = nc.tensor.transpose(bank[a][:, c * P:(c + 1) * P],
                                                         tile(kT if a < 2 else vT, 4 * (a % 2) + c), ident[:])
                            mm.then_inc(turned, 1)
                    if name == "first":
                        for a in range(2):
                            pe.wait_ge(v_ready, 2 * h + a + 1)
                            pe.wait_ge(xt_first, 2 * h + a + 1)
                            for c in range(4):
                                mm = nc.tensor.transpose(bank[2 + a][:, c * P:(c + 1) * P], xt[a][:, c, :], ident[:])
                            mm.then_inc(x_turned, 1)
                    if name == "out":
                        pe.wait_ge(kv_ready, 2 * h + 2)
                        if not first:
                            out_turn(h - 1, 1 - b)
                    if name == "level":
                        zb, xb = banks_of(k)[0:2], banks_of(k)[2:4]
                        if k == 0 and not first:
                            pe.wait_ge(y_done, 2 * h)
                        for a in range(2):
                            pe.wait_ge(lm_done, 2 * (NL + 1) * h + 2 * (k + 1) + a + 1)
                            if k == 0:
                                pe.wait_ge(x_first, 2 * h + a + 1)
                            else:
                                pe.wait_ge(x_up, X_UPS * h + 4 * (k - 1) + 2 * a + 2)
                            for c in range(4):
                                if k < NL - 1 or c == 0:
                                    mm = nc.tensor.matmul(bank[zb[a]][:, c * P:(c + 1) * P],
                                                          lm[(k + 1) % 2][a][:, c, :], xx[a][:, c, :], start=True,
                                                          stop=True)
                                else:
                                    mm = nc.tensor.matmul(bank[zb[a]][HC:P, c * P:c * P + HC],
                                                          lm[(k + 1) % 2][a][0:HC, c, HC:P], xx[a][0:HC, c, 0:HC],
                                                          start=True, stop=True)
                            mm.then_inc(z_done, 1)
                        for a in range(2):
                            pe.wait_ge(z_ready, 2 * NL * h + 2 * k + a + 1)
                            if k < NL - 1:
                                for c in range(4):
                                    nc.tensor.matmul(bank[xb[a][0]][:, c * P:(c + 1) * P], xt[a][:, c, :],
                                                     zz[a][:, c, :], start=True, stop=True)
                            for c in range(4):
                                if k < NL - 1 or c == 0:
                                    mm = nc.tensor.matmul(bank[xb[a][1]][:, c * P:(c + 1) * P], zz[a][:, c, :],
                                                          xt[a][:, c, :], start=True, stop=True)
                                else:
                                    mm = nc.tensor.matmul(bank[xb[a][1]][0:HC, c * P + HC:(c + 1) * P],
                                                          zz[a][HC:P, c, 0:HC], xt[a][HC:P, c, HC:P], start=True,
                                                          stop=True)
                            mm.then_inc(x_done, 1)
                    if name == "read" and k > 0:
                        pe.wait_ge(state_ready, (NC - 1) * h + k)
                        nc.tensor.matmul(bank[0][:, 0:P], tile(kT, k), state[:], start=True, stop=True) \
                            .then_inc(read_done, 1)
                        if k > 1:
                            pe.wait_ge(o1_ready, (NC - 1) * h + k - 1)
                        nc.tensor.matmul(bank[1][:, 0:P], tile(qT, k), state[:], start=True, stop=True) \
                            .then_inc(read_done, 1)
                    if name == "solve":
                        if k == 0:
                            pe.wait_ge(x_up, X_UPS * (h + 1))
                        else:
                            pe.wait_ge(rhs_ready, (NC - 1) * h + k)
                            pe.wait_ge(o_ready, NC * h + k)
                        nc.tensor.matmul(bank[2][:, 0:P], xt[k // 4][:, k % 4, :], vo[:, 0, :] if k == 0 else rhs[:],
                                         start=True, stop=True).then_inc(solved, 1)
                    if name == "update":
                        pe.wait_ge(w_ready, NC * h + k + 1)
                        if k == STATS_CHUNK and not (isinstance(h, int) and h == NH - 1):
                            pe.wait_ge(stat_step, 5 * h + 6)
                        if k < NC - 1:
                            nc.tensor.matmul(bank[3][:, 0:P], kd[:, k, :], wsol[:], start=True, stop=True) \
                                .then_inc(state_sum, 1)
                        nc.tensor.matmul(bank[2][:, P:2 * P], et[:, k, :], wsol[:], start=True, stop=True) \
                            .then_inc(attn_done, 1)

                def stats(h):
                    for a, src in ((0, 2), (1, 3)):
                        pe.wait_ge(sq_done, 2 * h + a + 1)
                        for c in range(NC):
                            mm = nc.tensor.matmul(bank[3][:, a * NC + c:a * NC + c + 1],
                                                  yT[:, src, c * C:(c + 1) * C], ones_col, start=True, stop=True)
                    mm.then_inc(stats_done, 1)

                def out_turn(h, b):
                    for a in range(2):
                        pe.wait_ge(o_scaled, 2 * h + a + 1)
                        for c in range(4):
                            mm = nc.tensor.transpose(bank[a][:, c * P:(c + 1) * P], vos[b][:, 4 * a + c, :], ident[:])
                        mm.then_inc(o_turned, 1)

                ones_col = triu[:, P - 1:P]

                def slot(h, b):
                    done = 0
                    free = dn_free(h + 1)
                    for name, k, fill in STEPS:
                        step(name, k, h, b)
                        pieces(done, fill, QKVZ * (h + 1), free)
                        done += fill

                pieces(0, 3 * BLOCK_PIECES, 0, dn_free(0))
                stats(0)
                pieces(3 * BLOCK_PIECES, BLOCK_PIECES, 0, dn_free(0))
                slot(0, 0)
                with pe.Fori(0, (NH - 2) // 2) as p:
                    slot(2 * p + 1, 1)
                    slot(2 * p + 2, 0)
                done = 0
                for s, (name, k, fill) in enumerate(STEPS):
                    if name != "stats":
                        step(name, k, NH - 1, 1)
                    n = min(fill, 2 * BLOCK_PIECES - done)
                    if s == len(STEPS) - 1:
                        n = 2 * BLOCK_PIECES - done
                    pieces(done, n, DN_BLOCKS, lru_free(0))
                    done += n

                pe.wait_ge(o_ready, NC * NH)
                out_turn(NH - 1, 1)

                def lru_gates(l, b):
                    pe.wait_ge(tapped, 3 * (DN_CONVS + l + 1))
                    pe.wait_ge(wg_loaded[b], 16 * (l - b + 2))
                    if isinstance(l, int) and l == 0:
                        pe.wait_ge(y_done, 2 * NH)
                    else:
                        pe.wait_ge(lru_dve, LD * l - 3)
                    for k in range(2):
                        if k == 1 and not (isinstance(l, int) and l == 0):
                            pe.wait_ge(lru_dve, LD * l)
                        for f in range(2):
                            mm = nc.tensor.matmul(bank[2 * k + f][:], wg[b][:, k, :],
                                                  qkv[b][0][:, HALF * f:HALF * (f + 1)], start=True, stop=True)
                        mm.then_inc(lgate_done, 1)

                def lru_stats(l, b):
                    pe.wait_ge(lru_act, LA * l + 7)
                    for c in range(NC):
                        mm = nc.tensor.matmul(bank[0][:, c:c + 1], qkv[b][1][:, c * C:(c + 1) * C], ones_col,
                                              start=True, stop=True)
                    mm.then_inc(lstat_done, 1)

                def lru_cast(l):
                    pe.wait_ge(lru_dve, LD * l + 4)
                    for c in range(NC):
                        mm = nc.tensor.matmul(bank[2 + c // 4][:, c % 4 * P:(c % 4 + 1) * P],
                                              small[:, 7, c:c + 1].to_broadcast([P, P]), ident[:], start=True,
                                              stop=True)
                    mm.then_inc(lcast_done, 1)

                def lru(l, b):
                    n0 = DN_BLOCKS + 2 * l
                    pieces(0, BLOCK_PIECES * 3 // 2, n0, lru_free(l))
                    lru_stats(l - 1, 1 - b)
                    pieces(BLOCK_PIECES * 3 // 2, BLOCK_PIECES // 2, n0, lru_free(l))
                    lru_cast(l - 1)
                    lru_gates(l, b)

                lru_gates(0, 0)
                with pe.Fori(0, (NH - 2) // 2) as p:
                    lru(2 * p + 1, 1)
                    lru(2 * p + 2, 0)
                lru(NH - 1, 1)
                lru_stats(NH - 1, 1)
                lru_cast(NH - 1)


def output_block(nc, env, st):
    x, w_out, final_norm_w, out, yT, w_hi, w_lo = (
        env[k] for k in "x w_out final_norm_w out yT hT_hi hT_lo".split())
    KE = 2 * D // P
    SPLITS = 4

    def sb(name, shape, dt=F32):
        return st.enter_context(nc.sbuf_tensor(name, shape, dt))

    def ps(name, shape):
        return st.enter_context(nc.psum_tensor(name, shape, F32))

    def sem(name):
        return st.enter_context(nc.semaphore(name))

    res = sb("res", [P, NC, D])
    stage = sb("stage", [P, 2, SPLITS // 2, HALF])
    y_hi = [sb(f"y_hi{i}", [P, KE, P], F32R) for i in range(2)]
    y_lo = [sb(f"y_lo{i}", [P, KE, P], F32R) for i in range(2)]
    fnw = sb("fnw", [P, D])
    rms = sb("rms3", [P, 3, NC])
    wh = w_hi[:].rearrange("p t s -> p (t s)").rearrange("p (e d) -> p e d", d=HALF)
    wl = w_lo[:].rearrange("p t s -> p (t s)").rearrange("p (e d) -> p e d", d=HALF)
    po = [ps(f"po{i}", [P, HALF]) for i in range(2)]
    NS = KE // 2

    x_in = sem("x_in")
    fnw_in = sem("fnw_in")
    stage_in = [sem(f"stage_in{i}") for i in range(2)]
    wo_hi = sem("wo_hi")
    wo_lo = sem("wo_lo")
    yh_done = sem("yh_done")
    yl_done = sem("yl_done")
    out_done = sem("out_done")
    added = sem("added")
    sq_done = sem("sq_done3")
    mean_done = sem("mean_done3")
    root_done = sem("root_done3")
    rec_done = sem("rec_done3")
    normed = sem("normed")
    stored = sem("stored")
    xt = x[0].rearrange("(n p) d -> p n d", p=P)
    ot = out[0].rearrange("(n p) d -> n p d", p=P)
    wv = w_out[0].rearrange("(e p) d -> p e d", p=P)

    with nc.Block() as block:
        @block.sync
        def _(sp):
            def load(f, n, b):
                sp.dma_start(stage[:, b], wv[:, bass.ds(2 * n, 2), bass.ds(HALF * f, HALF)]) \
                    .then_inc(stage_in[b], 16)

            for b in range(2):
                load(0, b, b)
            with sp.Fori(1, NS // 2) as m:
                for b in range(2):
                    sp.wait_ge(wo_lo, 2 * m + b - 1)
                    load(0, 2 * m + b, b)
            sp.dma_start(res[:], xt).then_inc(x_in, 16)
            sp.dma_start(fnw[:], final_norm_w.rearrange("(o d) -> o d", o=1).to_broadcast([P, D])) \
                .then_inc(fnw_in, 16)
            with sp.Fori(0, NS // 2) as m:
                for b in range(2):
                    sp.wait_ge(wo_lo, NS + 2 * m + b - 1)
                    load(1, 2 * m + b, b)
            with sp.Fori(0, NC) as t:
                sp.wait_ge(normed, 2 * t + 2)
                sp.dma_start(ot[bass.ds(t, 1)].rearrange("o p d -> p (o d)"),
                             res[:, bass.ds(t, 1), :].rearrange("p o d -> p (o d)")).then_inc(stored, 16)
            sp.wait_ge(stored, 16 * NC)

        @block.scalar
        def _(act):
            def w_split(f, m, b):
                act.wait_ge(stage_in[b], 16 * (NS // 2 * f + m + 1))
                if f == 1:
                    act.wait_ge(out_done, NC)
                nc.scalar.activation(wh[:, bass.ds(4 * m + 2 * b, 2), :], stage[:, b], ACT.Copy).then_inc(wo_hi, 1)

            def y_split(f, t, b):
                n = NC * f + t
                if not (isinstance(n, int) and n < 2):
                    act.wait_ge(out_done, n - 1)
                nc.scalar.activation(y_hi[b][:], yT[:, :, bass.ds(t * P, P)], ACT.Copy).then_inc(yh_done, 1)

            y_split(0, 0, 0)
            with act.Fori(0, NS // 2) as m:
                w_split(0, m, 0)
                w_split(0, m, 1)
            y_split(0, 1, 1)
            with act.Fori(1, NC // 2) as u:
                y_split(0, 2 * u, 0)
                y_split(0, 2 * u + 1, 1)
            y_split(1, 0, 0)
            with act.Fori(0, NS // 2) as m:
                w_split(1, m, 0)
                w_split(1, m, 1)
            y_split(1, 1, 1)

            def square(t):
                act.wait_ge(added, NC + t + 1)
                nc.scalar.activation(fsq, res[:, bass.ds(t, 1), :].rearrange("p o d -> p (o d)"), ACT.Square,
                                     accum_out=rms[:, 0, bass.ds(t, 1)]).then_inc(sq_done, 1)
                act.wait_ge(mean_done, t + 1)
                nc.scalar.activation(rms[:, 1, bass.ds(t, 1)], rms[:, 0, bass.ds(t, 1)], ACT.Sqrt) \
                    .then_inc(root_done, 1)

            fsq = stage[:].rearrange("p a b d -> p (a b d)")[:, 0:D]
            with act.Fori(1, NC // 2) as u:
                for b in range(2):
                    y_split(1, 2 * u + b, b)
                    square(2 * u + b - 2)
            square(NC - 2)
            square(NC - 1)

        @block.vector
        def _(dve):
            def y_split(f, t, b):
                dve.wait_ge(yh_done, NC * f + t + 1)
                nc.vector.tensor_tensor(y_lo[b][:], yT[:, :, bass.ds(t * P, P)], y_hi[b][:].bitcast(F32),
                                        ALU.subtract).then_inc(yl_done, 1)

            def add(f, t, b):
                dve.wait_ge(out_done, NC * f + t + 1)
                r = res[:, bass.ds(t, 1), HALF * f:HALF * (f + 1)]
                nc.vector.tensor_tensor(r, po[b][:].rearrange("p (o d) -> p o d", o=1), r, ALU.add) \
                    .then_inc(added, 1)

            def norm(t):
                dve.wait_ge(sq_done, t + 1)
                nc.vector.tensor_scalar(rms[:, 0, bass.ds(t, 1)], rms[:, 0, bass.ds(t, 1)], 1.0 / D, EPS,
                                        ALU.mult, ALU.add).then_inc(mean_done, 1)
                dve.wait_ge(root_done, t + 1)
                nc.vector.reciprocal(rms[:, 2, bass.ds(t, 1)], rms[:, 1, bass.ds(t, 1)]).then_inc(rec_done, 1)
                dve.wait_ge(rec_done, t + 1)
                r = res[:, bass.ds(t, 1), :].rearrange("p o d -> p (o d)")
                nc.vector.scalar_tensor_tensor(out=r, in0=r, scalar=rms[:, 2, bass.ds(t, 1)], in1=fnw[:],
                                               op0=ALU.mult, op1=ALU.mult).then_inc(normed, 2)

            y_split(0, 0, 0)
            y_split(0, 1, 1)
            dve.wait_ge(x_in, 16)
            with dve.Fori(1, NC // 2) as u:
                for b in range(2):
                    add(0, 2 * u + b - 2, b)
                    y_split(0, 2 * u + b, b)
            add(0, NC - 2, 0)
            y_split(1, 0, 0)
            add(0, NC - 1, 1)
            y_split(1, 1, 1)
            dve.wait_ge(fnw_in, 16)
            with dve.Fori(1, NC // 2) as u:
                for b in range(2):
                    add(1, 2 * u + b - 2, b)
                    y_split(1, 2 * u + b, b)
                    norm(2 * u + b - 2)
            for t in (NC - 2, NC - 1):
                add(1, t, t % 2)
                norm(t)

        @block.gpsimd
        def _(pool):
            for f in range(2):
                with pool.Fori(0, NS // 2) as m:
                    for b in range(2):
                        pool.wait_ge(wo_hi, NS * f + 2 * m + b + 1)
                        nc.gpsimd.tensor_tensor(wl[:, bass.ds(4 * m + 2 * b, 2), :], stage[:, b],
                                                wh[:, bass.ds(4 * m + 2 * b, 2), :].bitcast(F32),
                                                ALU.subtract).then_inc(wo_lo, 1)

        @block.tensor
        def _(pe):
            def tile(f, t, b, first):
                pe.wait_ge(yl_done, NC * f + t + 1)
                if not first:
                    pe.wait_ge(added, NC * f + t - 1)
                for n, (a, w) in enumerate(((y_hi, wh), (y_hi, wl), (y_lo, wh))):
                    for e in range(KE):
                        mm = nc.tensor.matmul(po[b][:], a[b][:, e, :], w[:, e, :], start=(n == 0 and e == 0),
                                              stop=(n == PASSES - 1 and e == KE - 1))
                mm.then_inc(out_done, 1)

            for f in range(2):
                pe.wait_ge(wo_lo, NS * (f + 1))
                if f == 0:
                    tile(0, 0, 0, True)
                    tile(0, 1, 1, True)
                with pe.Fori(1 - f, NC // 2) as u:
                    tile(f, 2 * u, 0, False)
                    tile(f, 2 * u + 1, 1, False)


_INS = ['x', 'norm_w', 'w_in', 'lru_conv_w', 'lru_conv_b', 'lru_wa', 'lru_ba', 'lru_wx', 'lru_bx', 'lru_lambda',
        'lru_norm_w', 'dn_conv_w', 'dn_A_log', 'dn_dt_bias', 'dn_norm_w', 'w_out', 'final_norm_w']


def kernel(**inputs):
    import numpy as _np
    import concourse.bacc as _bacc
    from concourse import mybir as _mybir
    from concourse.bass_utils import run_bass_kernel_spmd as _run

    nc = _bacc.Bacc("TRN2", target_bir_lowering=False, num_devices=1)
    arrays, args = {}, []
    for name in _INS:
        a = _np.ascontiguousarray(inputs[name])
        arrays[f"in_{name}_dram"] = a
        args.append(nc.dram_tensor(f"in_{name}_dram", a.shape, _mybir.dt.from_np(a.dtype), kind="ExternalInput").ap())
    args.append(nc.dram_tensor("out_0_dram", (1, S, D), _mybir.dt.float32, kind="ExternalOutput").ap())
    build(nc, *args)
    r = _run(nc, [arrays], core_ids=[0])
    return r.results[0]["out_0_dram"]
```

```python
from contextlib import ExitStack

import concourse.bass as bass
from concourse import mybir

ALU = mybir.AluOpType
ACT = mybir.ActivationFunctionType
F32 = mybir.dt.float32
F32R = mybir.dt.float32r

P = 128
S = 1024
D = 1024
KT = D // P
C = 128
NC = S // C
NH = 8
HALF = 512
TAPS = 4
EPS = 1e-6
LRU_C = 8.0
QKVZ = 4
PASSES = 3
PIECE = 4
BLOCK_PIECES = 2 * KT * PASSES // PIECE
LEVELS = [2, 4, 8, 16, 32, 64]
COL_DN = 2 * D
COL_AB = COL_DN + QKVZ * D
QUARTER = 4
SERIES = 8

NORM_W = 0
LRU_TAP = NORM_W + KT
LRU_B = LRU_TAP + TAPS * NH
LRU_BA = LRU_B + NH
LRU_BX = LRU_BA + NH
LRU_LAM = LRU_BX + NH
LRU_NW = LRU_LAM + NH
DN_NW = LRU_NW + NH
ROWS_A = DN_NW + 1
DN_TAP = P
ROWS_B = TAPS * 3 * NH

CHAIN = ("read", "solve", "update")
STATS_CHUNK = 5
STEPS = (
    [("scores", 0, 7), ("turn", 0, 4), ("first", 0, 4), ("out", 0, 4)]
    + [("level", k, f) for k, f in enumerate((2, 2, 1, 1, 0, 0))]
    + [("read", 0, 0), ("solve", 0, 1), ("update", 0, 1)]
    + [(name, c, 1) for c in range(1, STATS_CHUNK) for name in CHAIN]
    + [("read", STATS_CHUNK, 1), ("stats", 0, 0), ("solve", STATS_CHUNK, 1), ("update", STATS_CHUNK, 1)]
    + [(name, c, 1) for c in range(STATS_CHUNK + 1, NC) for name in CHAIN]
    + [("tail", 0, 0)]
)
assert sum(fill for _, _, fill in STEPS) == QKVZ * BLOCK_PIECES


def done_at(blocks):
    ends, pieces, j = [], 0, 0
    for n, (_, _, fill) in enumerate(STEPS):
        pieces += fill * blocks // QKVZ if blocks == QKVZ else fill
        ends.append([])
        while j < blocks and (pieces >= (j + 1) * BLOCK_PIECES or n == len(STEPS) - 1):
            ends[-1].append(j)
            j += 1
    return ends


def tap_steps(done):
    out = []
    for j in range(3):
        s = next(n for n, ends in enumerate(done) if j in ends)
        steps = range(s, len(STEPS)) if j < 2 else [n for n in range(s, len(STEPS)) if STEPS[n][0] == "read"]
        out.append(list(steps)[:TAPS - 1])
    return out


def build(nc, x, norm_w, w_in, lru_conv_w, lru_conv_b, lru_wa, lru_ba, lru_wx, lru_bx, lru_lambda,
          lru_norm_w, dn_conv_w, dn_A_log, dn_dt_bias, dn_norm_w, w_out, final_norm_w, out):
    gc_rows = nc.dram_tensor("gc_rows", [NH * NC, C], F32).ap()
    w_in_v = w_in[0].rearrange("(t p) e -> p t e", p=P)
    keep = ExitStack()
    with keep:
        def sb(name, shape, dt=F32, stack=keep):
            return stack.enter_context(nc.sbuf_tensor(name, shape, dt))

        def sem(name, stack=keep):
            return stack.enter_context(nc.semaphore(name))

        yT = sb("yT", [P, 2 * NH, S])
        hT_hi = sb("hT_hi", [P, KT, S], F32R)
        hT_lo = sb("hT_lo", [P, KT, S], F32R)
        with ExitStack() as mix:
            ident = sb("ident", [P, P], stack=mix)
            par = sb("par", [P, P + ROWS_B], stack=mix)
            beta = sb("beta", [P, NH, NC], stack=mix)
            gc = sb("gc", [P, NH, NC], stack=mix)
            egc = sb("egc", [P, NH, NC], stack=mix)
            negegc = sb("negegc", [P, NH, NC], stack=mix)
            eglast = sb("eglast", [P, NH, NC], stack=mix)
            ekd = sb("ekd", [P, NH, NC], stack=mix)
            sp8 = sb("sp8", [P, 2, NH], stack=mix)
            triu = sb("triu", [P, P], stack=mix)
            masks = sb("masks", [P, 1 + len(LEVELS), P], stack=mix)

            w_raw = [sb(f"w_raw{i}", [P, KT, P], stack=mix) for i in range(2)]
            w_hi = [sb(f"w_hi{i}", [P, KT, P], F32R, stack=mix) for i in range(2)]
            w_lo = [sb(f"w_lo{i}", [P, KT, P], F32R, stack=mix) for i in range(2)]
            pp = [mix.enter_context(nc.psum_tensor(f"pp{i}", [P, S], F32)) for i in range(2)]
            w_loaded = [sem(f"w_loaded{i}", mix) for i in range(2)]
            hi_split = sem("hi_split", mix)
            lo_split = sem("lo_split", mix)
            projected = sem("projected", mix)

            first_block(nc, locals())
            mixer_block(nc, locals())
        with ExitStack() as last:
            output_block(nc, locals(), last)


def first_block(nc, env):
    (x, w_in_v, gc_rows, ident, par, beta, gc, egc, negegc, eglast, ekd, sp8, triu, masks, hT_hi, hT_lo) = (
        env[k] for k in "x w_in_v gc_rows ident par beta gc egc negegc eglast ekd sp8 triu masks hT_hi hT_lo".split())
    w_raw, w_hi, w_lo, pp, w_loaded, hi_split, lo_split, projected = (
        env[k] for k in "w_raw w_hi w_lo pp w_loaded hi_split lo_split projected".split())
    GATES = NH * NC
    GATE_STEPS = 15 + SERIES
    with ExitStack() as st:
        def sb(name, shape, dt=F32):
            return st.enter_context(nc.sbuf_tensor(name, shape, dt))

        def ps(name, shape):
            return st.enter_context(nc.psum_tensor(name, shape, F32))

        def sem(name):
            return st.enter_context(nc.semaphore(name))

        xs = env["yT"][:, 0:NC, :]
        junk = sb("junk", [P, 2, D])
        h32 = sb("h32", [P, 2, KT, P])
        rowsA = sb("rowsA", [ROWS_A, P])
        rowsB = sb("rowsB", [ROWS_B, P])
        ones = sb("ones", [P, P])
        rms = sb("rms", [P, 3, NC])
        wab = sb("wab", [P, KT, 2 * NH])
        wab_hi = sb("wab_hi", [P, KT, 2 * NH], F32R)
        wab_lo = sb("wab_lo", [P, KT, 2 * NH], F32R)
        alog = sb("alog", [P, 2, NH])
        aexp = sb("aexp", [P, NH])
        xcat = sb("xcat", [P, GATES + NH])
        sp = sb("sp", [P, 8, GATES + NH])
        g = sb("g", [P, NH, NC])
        gcrow_sb = sb("gcrow_sb", [GATES, C])
        tr = [pp[i][:].rearrange("p (f s) -> p f s", f=2) for i in range(2)]
        pab = ps("pab", [P, NC, 2 * NH])
        ppar = ps("ppar", [P, HALF])
        abT = sb("abT", [2 * NH, S])
        pgc = ps("pgc", [P, HALF])
        pgl = ps("pgl", [P, HALF])
        pabT = [ppar, pgl]

        x_loaded = [sem(f"x_loaded{i}") for i in range(NC)]
        rows_loaded = sem("rows_loaded")
        wab_loaded = sem("wab_loaded")
        alog_loaded = sem("alog_loaded")
        const = sem("const")
        squared = sem("squared")
        mean_done = sem("mean_done")
        root_done = sem("root_done")
        rms_done = sem("rms_done")
        x_scaled = sem("x_scaled")
        turned = sem("turned")
        h_ready = sem("h_ready")
        hi_ready = sem("hi_ready")
        lo_ready = sem("lo_ready")
        par_turned = sem("par_turned")
        par_ready = sem("par_ready")
        wab_split = sem("wab_split")
        ab_done = sem("ab_done")
        ab_copied = sem("ab_copied")
        ab_turned = sem("ab_turned")
        gate_act = sem("gate_act")
        gate_dve = sem("gate_dve")
        gate_pe = sem("gate_pe")
        rows_stored = sem("rows_stored")
        xt = x[0].rearrange("(n p) d -> n p d", p=P)

        with nc.Block() as block:
            @block.sync
            def _(sp_eng):
                for t in range(3):
                    sp_eng.dma_start(xs[:, t, :], xt[t]).then_inc(x_loaded[t], 16)
                n = 0
                for name, rows in (("norm_w", KT), ("lru_conv_w", TAPS * NH), ("lru_conv_b", NH), ("lru_ba", NH),
                                   ("lru_bx", NH), ("lru_lambda", NH), ("lru_norm_w", NH), ("dn_norm_w", 1)):
                    src = env[name]
                    src = src.rearrange("o k (b p) -> (o k b) p", p=P) if len(src.shape) == 3 else \
                        src.rearrange("o (b p) -> (o b) p", p=P)
                    sp_eng.dma_start(rowsA[n:n + rows, :], src).then_inc(rows_loaded, 16)
                    n += rows
                sp_eng.dma_start(rowsB[:], env["dn_conv_w"].rearrange("o k (b p) -> (o k b) p", p=P)) \
                    .then_inc(rows_loaded, 16)
                sp_eng.dma_start(wab[:], w_in_v[:, :, COL_AB:COL_AB + 2 * NH]).then_inc(wab_loaded, 16)
                sp_eng.dma_start(alog[:, 0, :], env["dn_A_log"].to_broadcast([P, NH])).then_inc(alog_loaded, 16)
                sp_eng.dma_start(alog[:, 1, :], env["dn_dt_bias"].to_broadcast([P, NH])).then_inc(alog_loaded, 16)
                for t in range(3, NC):
                    sp_eng.dma_start(xs[:, t, :], xt[t]).then_inc(x_loaded[t], 16)
                for j in range(2):
                    sp_eng.dma_start(w_raw[j][:], w_in_v[:, :, COL_DN + j * D:COL_DN + j * D + P]) \
                        .then_inc(w_loaded[j], 16)
                for j in range(2, QKVZ):
                    sp_eng.wait_ge(lo_split, j - 1)
                    sp_eng.dma_start(w_raw[j % 2][:], w_in_v[:, :, COL_DN + j * D:COL_DN + j * D + P]) \
                        .then_inc(w_loaded[j % 2], 16)
                sp_eng.wait_ge(gate_act, 6)
                sp_eng.dma_start(gc_rows, gcrow_sb[:]).then_inc(rows_stored, 16)
                sp_eng.wait_ge(rows_stored, 16)

            @block.gpsimd
            def _(pool):
                nc.gpsimd.memset(ident[:], 0.0)
                nc.gpsimd.memset(ones[:], 1.0).then_inc(const, 1)
                pool.wait_ge(const, 1)
                nc.gpsimd.affine_select(out=ident[:], in_=ident[:], compare_op=ALU.not_equal, fill=1.0, base=0,
                                        pattern=[[-1, P]], channel_multiplier=1)
                nc.gpsimd.affine_select(out=triu[:], in_=ones[:], compare_op=ALU.is_ge, fill=0.0, base=0,
                                        pattern=[[1, P]], channel_multiplier=-1).then_inc(const, 1)
                pool.wait_ge(wab_split, 1)
                nc.gpsimd.tensor_tensor(wab_lo[:], wab[:], wab_hi[:].bitcast(F32), ALU.subtract).then_inc(wab_split, 1)
                for t in range(NC):
                    pool.wait_ge(hi_ready, t + 1)
                    nc.gpsimd.tensor_tensor(hT_lo[:, :, t * P:(t + 1) * P], h32[:, t % 2],
                                            hT_hi[:, :, t * P:(t + 1) * P].bitcast(F32),
                                            ALU.subtract).then_inc(lo_ready, 1)
                    if t >= NC - 2:
                        j = t - (NC - 2)
                        pool.wait_ge(hi_split, j + 1)
                        nc.gpsimd.tensor_tensor(w_lo[j][:], w_raw[j][:], w_hi[j][:].bitcast(F32), ALU.subtract) \
                            .then_inc(lo_split, 1)
                nc.gpsimd.memset(masks[:], -1.0).then_inc(const, 1)
                pool.wait_ge(const, 3)
                n = 3
                for lv, b in enumerate([1] + LEVELS):
                    m = masks[:, lv, :].rearrange("p (n s b) -> p n s b", s=2, b=b)
                    for base, mult, step, fill_s in ((0, 1, -2 * b, None), (b - 1, -1, 2 * b, None)):
                        nc.gpsimd.affine_select(out=m, in_=m, compare_op=ALU.is_ge, fill=0.0, base=base,
                                                pattern=[[step, P // (2 * b)], [0, 2], [0, b]],
                                                channel_multiplier=mult).then_inc(const, 1)
                        n += 1
                        pool.wait_ge(const, n)
                    nc.gpsimd.memset(m[:, :, 0, :], 0.0).then_inc(const, 1)
                    n += 1
                    pool.wait_ge(const, n)
                pool.wait_ge(hi_split, 3)
                nc.gpsimd.tensor_tensor(w_lo[0][:], w_raw[0][:], w_hi[0][:].bitcast(F32), ALU.subtract) \
                    .then_inc(lo_split, 1)

            @block.scalar
            def _(act):
                def square(t):
                    act.wait_ge(x_loaded[t], 16)
                    nc.scalar.activation(junk[:, t % 2], xs[:, t, :], ACT.Square,
                                         accum_out=rms[:, 0, t:t + 1]).then_inc(squared, 1)

                def root(t):
                    act.wait_ge(mean_done, t + 1)
                    nc.scalar.activation(rms[:, 1, t:t + 1], rms[:, 0, t:t + 1], ACT.Sqrt).then_inc(root_done, 1)

                def h_high(t):
                    act.wait_ge(h_ready, 2 * (t + 1))
                    nc.scalar.activation(hT_hi[:, :, t * P:(t + 1) * P], h32[:, t % 2], ACT.Copy).then_inc(hi_ready, 1)

                def w_high(j):
                    act.wait_ge(w_loaded[j], 16)
                    nc.scalar.activation(w_hi[j][:], w_raw[j][:], ACT.Copy).then_inc(hi_split, 1)

                square(0)
                square(1)
                root(0)
                for t in range(NC):
                    if t + 2 < NC:
                        square(t + 2)
                    if t + 1 < NC:
                        root(t + 1)
                    if t == 0:
                        act.wait_ge(wab_loaded, 16)
                        nc.scalar.activation(wab_hi[:], wab[:], ACT.Copy).then_inc(wab_split, 1)
                    if t >= 1:
                        h_high(t - 1)
                    if t == NC - 1:
                        w_high(0)
                h_high(NC - 1)
                w_high(1)
                act.wait_ge(gate_dve, 2)
                nc.scalar.activation(sp[:, 0, :], xcat[:], ACT.Abs).then_inc(gate_act, 1)
                act.wait_ge(gate_act, 1)
                nc.scalar.activation(sp[:, 1, :], sp[:, 0, :], ACT.Exp, scale=-1.0).then_inc(gate_act, 1)
                act.wait_ge(alog_loaded, 32)
                nc.scalar.activation(aexp[:], alog[:, 0, :], ACT.Exp).then_inc(gate_act, 1)
                nc.scalar.activation(beta[:].rearrange("p h c -> p c h"), pab[:, :, 0:NH], ACT.Sigmoid) \
                    .then_inc(gate_act, 1)
                act.wait_ge(projected, 1)
                act.wait_ge(w_loaded[0], 32)
                nc.scalar.activation(w_hi[0][:], w_raw[0][:], ACT.Copy).then_inc(hi_split, 1)
                act.wait_ge(gate_pe, 2)
                nc.scalar.activation(egc[:], pgc[:, 0:GATES].rearrange("p (h c) -> p h c", h=NH), ACT.Exp) \
                    .then_inc(gate_act, 1)
                nc.scalar.activation(gcrow_sb[:], pgc[0:GATES, P:2 * P], ACT.Copy).then_inc(gate_act, 1)
                act.wait_ge(gate_pe, 3)
                nc.scalar.activation(eglast[:], pgl[:, 0:GATES].rearrange("p (h c) -> p h c", h=NH), ACT.Exp) \
                    .then_inc(gate_act, 1)
                act.wait_ge(gate_dve, GATE_STEPS)
                nc.scalar.activation(ekd[:], ekd[:], ACT.Exp).then_inc(gate_act, 1)

            @block.vector
            def _(dve):
                def evacuate(t):
                    for f in range(2):
                        dve.wait_ge(turned, t + 1)
                        if f == 0 and t >= 2:
                            dve.wait_ge(lo_ready, t - 1)
                        nc.vector.tensor_tensor(
                            h32[:, t % 2, 4 * f:4 * f + 4, :], tr[t % 2][:, f, :].rearrange("p (d s) -> p d s", s=P),
                            par[:, NORM_W + 4 * f:NORM_W + 4 * f + 4].unsqueeze(2).to_broadcast([P, 4, P]),
                            ALU.mult).then_inc(h_ready, 1)

                def mean(t):
                    dve.wait_ge(squared, t + 1)
                    nc.vector.tensor_scalar(rms[:, 0, t:t + 1], rms[:, 0, t:t + 1], 1.0 / D, EPS, ALU.mult,
                                            ALU.add).then_inc(mean_done, 1)

                mean(0)
                for t in range(NC):
                    if t + 1 < NC:
                        mean(t + 1)
                    dve.wait_ge(root_done, t + 1)
                    nc.vector.reciprocal(rms[:, 2, t:t + 1], rms[:, 1, t:t + 1]).then_inc(rms_done, 1)
                    dve.wait_ge(rms_done, t + 1)
                    nc.vector.tensor_scalar(xs[:, t, :], xs[:, t, :], rms[:, 2, t:t + 1], None,
                                            ALU.mult).then_inc(x_scaled, 1)
                    if t == 0:
                        dve.wait_ge(par_turned, 1)
                        nc.vector.tensor_copy(par[:, 0:ROWS_A], ppar[:, 0:ROWS_A])
                        nc.vector.tensor_copy(par[:, DN_TAP:], ppar[:, DN_TAP:DN_TAP + ROWS_B]).then_inc(par_ready, 1)
                        dve.wait_ge(par_ready, 1)
                    if t >= 1:
                        evacuate(t - 1)
                evacuate(NC - 1)
                nc.vector.tensor_scalar(xcat[:, GATES:], par[:, LRU_LAM:LRU_LAM + NH], -1.0, None, ALU.mult) \
                    .then_inc(gate_dve, 1)
                for f in range(2):
                    dve.wait_ge(ab_done, f + 1)
                    nc.vector.tensor_copy(abT[:, HALF * f:HALF * (f + 1)], pabT[f][0:2 * NH, :]) \
                        .then_inc(ab_copied, 1)
                dve.wait_ge(ab_turned, 1)
                dve.wait_ge(alog_loaded, 32)
                nc.vector.tensor_tensor(xcat[:, 0:GATES].rearrange("p (h c) -> p c h", h=NH), pab[:, :, NH:2 * NH],
                                        alog[:, 1, :].unsqueeze(1).to_broadcast([P, NC, NH]), ALU.add) \
                    .then_inc(gate_dve, 1)
                count = [2]

                def step(ins):
                    count[0] += 1
                    ins.then_inc(gate_dve, 1)
                    dve.wait_ge(gate_dve, count[0])

                z, den, s1, s2, acc = (sp[:, k, :] for k in (1, 2, 3, 4, 5))
                dve.wait_ge(gate_act, 2)
                step(nc.vector.tensor_scalar(den, z, 2.0, None, ALU.add))
                step(nc.vector.reciprocal(den, den))
                step(nc.vector.tensor_tensor(s1, z, den, ALU.mult))
                step(nc.vector.tensor_tensor(s2, s1, s1, ALU.mult))
                step(nc.vector.tensor_scalar(acc, s2, 1.0 / (2 * SERIES + 1), None, ALU.mult))
                for k in range(SERIES - 1, 0, -1):
                    step(nc.vector.scalar_tensor_tensor(out=acc, in0=acc, scalar=1.0 / (2 * k + 1), in1=s2,
                                                        op0=ALU.add, op1=ALU.mult))
                step(nc.vector.scalar_tensor_tensor(out=acc, in0=acc, scalar=1.0, in1=s1, op0=ALU.add, op1=ALU.mult))
                step(nc.vector.tensor_scalar(s2, xcat[:], 0.0, None, ALU.max))
                step(nc.vector.scalar_tensor_tensor(out=acc, in0=acc, scalar=2.0, in1=s2, op0=ALU.mult, op1=ALU.add))
                step(nc.vector.tensor_scalar(sp8[:, 0, :], acc[:, GATES:], LRU_C, None, ALU.mult))
                step(nc.vector.tensor_scalar(sp8[:, 1, :], acc[:, GATES:], -LRU_C, None, ALU.mult))
                dve.wait_ge(gate_act, 3)
                step(nc.vector.scalar_tensor_tensor(
                    out=g[:], in0=acc[:, 0:GATES].rearrange("p (h c) -> p h c", h=NH), scalar=-1.0,
                    in1=aexp[:].unsqueeze(2).to_broadcast([P, NH, NC]), op0=ALU.mult, op1=ALU.mult))
                dve.wait_ge(gate_pe, 3)
                dve.wait_ge(gate_act, 7)
                step(nc.vector.tensor_copy(gc[:], pgc[:, 0:GATES].rearrange("p (h c) -> p h c", h=NH)))
                step(nc.vector.tensor_scalar(negegc[:], egc[:], -1.0, None, ALU.mult))
                step(nc.vector.tensor_tensor(ekd[:], pgl[:, 0:GATES].rearrange("p (h c) -> p h c", h=NH), gc[:],
                                             ALU.subtract))
                assert count[0] == GATE_STEPS

            @block.tensor
            def _(pe):
                pe.wait_ge(const, 2)
                pe.wait_ge(rows_loaded, 16 * 9)
                nc.tensor.transpose(ppar[:, 0:ROWS_A], rowsA[:], ident[0:ROWS_A, 0:ROWS_A])
                nc.tensor.transpose(ppar[:, P:P + ROWS_B], rowsB[:], ident[0:ROWS_B, 0:ROWS_B]).then_inc(par_turned, 1)

                def gates(f):
                    if f == 0:
                        pe.wait_ge(par_ready, 1)
                        pe.wait_ge(wab_split, 2)
                    for d in range(KT):
                        for n, (a, b) in enumerate(((wab_hi, hT_hi), (wab_hi, hT_lo), (wab_lo, hT_hi))):
                            last = nc.tensor.matmul(pabT[f][0:2 * NH, :], a[:, d, :],
                                                    b[:, d, HALF * f:HALF * (f + 1)], start=(d == 0 and n == 0),
                                                    stop=(d == KT - 1 and n == PASSES - 1))
                    last.then_inc(ab_done, 1)

                def gates_turn():
                    pe.wait_ge(ab_copied, 2)
                    for t in range(NC):
                        last = nc.tensor.transpose(pab[:, t, :], abT[:, t * P:(t + 1) * P],
                                                   ident[0:2 * NH, 0:2 * NH])
                    last.then_inc(ab_turned, 1)

                for t in range(NC):
                    pe.wait_ge(x_scaled, t + 1)
                    if t >= 2:
                        pe.wait_ge(h_ready, 2 * (t - 1))
                    for d in range(KT):
                        last = nc.tensor.transpose(tr[t % 2][:, d // 4, (d % 4) * P:(d % 4 + 1) * P],
                                                   xs[:, t, d * P:(d + 1) * P], ident[:])
                    last.then_inc(turned, 1)
                    if t == NC - 2:
                        pe.wait_ge(lo_ready, NC // 2)
                        gates(0)
                pe.wait_ge(lo_ready, NC)
                gates(1)
                gates_turn()
                pe.wait_ge(h_ready, 2 * NC)
                for j in range(2):
                    pe.wait_ge(lo_split, j + 1)
                    for f in range(2):
                        for d in range(KT):
                            for n, (w, hh) in enumerate(((w_hi, hT_hi), (w_hi, hT_lo), (w_lo, hT_hi))):
                                last = nc.tensor.matmul(pp[j][:, HALF * f:HALF * (f + 1)], w[j][:, d, :],
                                                        hh[:, d, HALF * f:HALF * (f + 1)], start=(d == 0 and n == 0),
                                                        stop=(d == KT - 1 and n == PASSES - 1))
                    last.then_inc(projected, 1)
                    if j == 0:
                        pe.wait_ge(gate_dve, GATE_STEPS - 3)
                        gf = g[:].rearrange("p h c -> p (h c)")
                        nc.tensor.matmul(pgc[:, 0:GATES], triu[:], gf, start=True, stop=True).then_inc(gate_pe, 1)
                        nc.tensor.matmul(pgc[0:GATES, P:2 * P], gf, triu[:], start=True, stop=True).then_inc(gate_pe, 1)
                        nc.tensor.matmul(pgl[:, 0:GATES], ones[:], gf, start=True, stop=True).then_inc(gate_pe, 1)



def mixer_block(nc, env):
    (w_in_v, gc_rows, yT, ident, par, beta, gc, egc, negegc, eglast, ekd, sp8, triu, masks, hT_hi, hT_lo) = (
        env[k] for k in
        "w_in_v gc_rows yT ident par beta gc egc negegc eglast ekd sp8 triu masks hT_hi hT_lo".split())
    w_raw, w_hi, w_lo, pp, w_loaded, hi_split, lo_split, projected = (
        env[k] for k in "w_raw w_hi w_lo pp w_loaded hi_split lo_split projected".split())
    NL = len(LEVELS)
    HC = C // 2
    DN_BLOCKS = QKVZ * NH
    N_BLOCKS = DN_BLOCKS + 2 * NH
    DN_CONVS = 3 * NH
    X_UPS = 4 * (NL - 1) + 2
    with ExitStack() as st:
        def sb(name, shape, dt=F32):
            return st.enter_context(nc.sbuf_tensor(name, shape, dt))

        def ps(name, shape):
            return st.enter_context(nc.psum_tensor(name, shape, F32))

        def sem(name):
            return st.enter_context(nc.semaphore(name))

        qkv = [[sb(f"{n}T{i}", [P, S]) for n in "qkv"] for i in range(2)]
        kd = sb("kd", [P, NC, P])
        vos = [sb(f"vo{i}", [P, NC, P]) for i in range(2)]
        ets = [sb(f"et{i}", [P, NC, P]) for i in range(2)]
        qe = sb("qe", [P, 2, NC])
        state = sb("state", [P, P])
        rhs = sb("rhs", [P, P])
        wsol = sb("wsol", [P, P])
        o1 = sb("o1", [P, P])
        junk = sb("junk2", [P, P])
        sse = sb("sse", [P, 2, NC])
        small = sb("small", [P, 8, NC])
        seed = sb("seed", [P, 2])
        wg = [sb(f"wg{i}", [P, 2, P]) for i in range(2)]
        gt = yT[:, 2, :].rearrange("p (c i) -> p c i", i=P)
        xx = [yT[:, 3, HALF * b:HALF * (b + 1)].rearrange("p (c i) -> p c i", i=P) for b in range(2)]
        xt = [yT[:, 4, HALF * b:HALF * (b + 1)].rearrange("p (c i) -> p c i", i=P) for b in range(2)]
        zz = [yT[:, 5, HALF * b:HALF * (b + 1)].rearrange("p (c i) -> p c i", i=P) for b in range(2)]
        lm = [[yT[:, 6 + k, HALF * b:HALF * (b + 1)].rearrange("p (c i) -> p c i", i=P) for b in range(2)]
              for k in range(2)]
        bank = [ps(f"bank{i}", [P, HALF]) for i in range(4)]

        tap_first = sem("tap_first")
        tapped = sem("tapped")
        gated = sem("gated")
        rows_in = sem("rows_in")
        sq_done = sem("sq_done")
        stats_done = sem("stats_done")
        stat_step = sem("stat_step")
        root_n = sem("root_n")
        turned = sem("turned2")
        kv_ready = sem("kv_ready")
        v_ready = sem("v_ready")
        scored = sem("scored")
        gap_done = sem("gap_done")
        decay_exp = sem("decay_exp")
        et_done = sem("et_done")
        gt_done = sem("gt_done")
        attn_ready = sem("attn_ready")
        lm_done = sem("lm_done")
        xt_first = sem("xt_first")
        x_turned = sem("x_turned")
        x_first = sem("x_first")
        z_done = sem("z_done")
        z_ready = sem("z_ready")
        x_done = sem("x_done")
        x_up = sem("x_up")
        read_done = sem("read_done")
        rhs_ready = sem("rhs_ready")
        o1_ready = sem("o1_ready")
        solved = sem("solved")
        w_ready = sem("w_ready")
        state_sum = sem("state_sum")
        attn_done = sem("attn_done")
        state_ready = sem("state_ready")
        o_ready = sem("o_ready")
        o_squared = sem("o_squared")
        o_mean = sem("o_mean")
        o_root = sem("o_root")
        o_rec = sem("o_rec")
        o_scaled = sem("o_scaled")
        o_turned = sem("o_turned")
        y_done = sem("y_done")
        wg_loaded = [sem(f"wg_loaded{i}") for i in range(2)]
        lgate_done = sem("lgate_done")
        lru_act = sem("lru_act")
        lru_ix = sem("lru_ix")
        lru_dve = sem("lru_dve")
        lru_h = sem("lru_h")
        lstat_done = sem("lstat_done")
        lcast_done = sem("lcast_done")
        LA, LD = 8, 6

        w_out_v = env["w_out"][0].rearrange("(e p) d -> p e d", p=P)

        def flat(t):
            return t[:].rearrange("p k c -> p (k c)")

        DN_DONE = done_at(QKVZ)
        TAP_AT = tap_steps(DN_DONE)
        LRU_DONE = done_at(2)

        def column(j, h):
            return COL_DN + j * D + h * P

        def banks_of(level):
            p, q, r, s = 0, 1, 2, 3
            for _ in range(level):
                p, q, r, s = r, p, s, q
            return p, q, (r, s), (p, q)

        with nc.Block() as block:
            @block.sync
            def _(sp):
                def load(j, count, col, n):
                    sp.wait_ge(lo_split, n - 1)
                    sp.dma_start(w_raw[j % 2][:], w_in_v[:, :, bass.ds(col, P)]).then_inc(w_loaded[j % 2], 16)

                def head(h):
                    for j in range(QKVZ):
                        load(j, 0, column(j, h), QKVZ * h + j)

                with sp.Fori(1, NH) as h:
                    head(h)

                def gate_weights(l, b):
                    sp.dma_start(wg[b][:, 0, :], env["lru_wa"][0, bass.ds(l, 1)].rearrange("o i j -> i (o j)")) \
                        .then_inc(wg_loaded[b], 16)
                    sp.dma_start(wg[b][:, 1, :], env["lru_wx"][0, bass.ds(l, 1)].rearrange("o i j -> i (o j)")) \
                        .then_inc(wg_loaded[b], 16)

                def lru_head(l, b):
                    load(0, 0, l * P, DN_BLOCKS + 2 * l)
                    load(1, 0, D + l * P, DN_BLOCKS + 2 * l + 1)
                    if isinstance(l, int) and l < 2:
                        gate_weights(l, b)
                    else:
                        sp.wait_ge(lgate_done, 2 * (l - 1))
                        gate_weights(l, b)

                lru_head(0, 0)
                lru_head(1, 1)
                with sp.Fori(1, NH // 2) as p:
                    lru_head(2 * p, 0)
                    lru_head(2 * p + 1, 1)
                for i in range(QUARTER):
                    sp.wait_ge(lo_split, N_BLOCKS + i - 1)
                    sp.dma_start(flat(w_raw[i % 2]), w_out_v[:, i, :]).then_inc(w_loaded[i % 2], 16)

            @block.gpsimd
            def _(pool):
                def split(j, n):
                    pool.wait_ge(hi_split, n + 1)
                    nc.gpsimd.tensor_tensor(w_lo[j % 2][:], w_raw[j % 2][:], w_hi[j % 2][:].bitcast(F32),
                                            ALU.subtract).then_inc(lo_split, 1)

                def prepare(h, b):
                    q, kk, _ = qkv[b]
                    pool.wait_ge(gated, QKVZ * h + 2)
                    if not (isinstance(h, int) and h == 0):
                        pool.wait_ge(x_done, 2 * NL * h)
                        pool.wait_ge(z_ready, 2 * NL * h)
                    nc.gpsimd.tensor_tensor(yT[:, 2, :], kk[:], kk[:], ALU.mult).then_inc(sq_done, 1)
                    nc.gpsimd.tensor_tensor(yT[:, 3, :], q[:], q[:], ALU.mult).then_inc(sq_done, 1)
                    pool.wait_ge(rows_in, 16 * (h + 1))
                    nc.gpsimd.tensor_tensor(ets[b][:], gc[:, bass.ds(h, 1), :].rearrange("p o c -> p (o c)")
                                            .unsqueeze(2).to_broadcast([P, NC, P]), ets[b][:],
                                            ALU.subtract).then_inc(gap_done, 1)

                def weigh(h, b):
                    pool.wait_ge(decay_exp, 2 * h + 2)
                    nc.gpsimd.tensor_tensor(ets[b][:], ets[b][:], triu[:].unsqueeze(1).to_broadcast([P, NC, P]),
                                            ALU.mult).then_inc(et_done, 1)
                    pool.wait_ge(stat_step, 5 * h + 3)
                    pool.wait_ge(et_done, 2 * h + 1)
                    nc.gpsimd.tensor_tensor(ets[b][:], ets[b][:], small[:, 2, :].unsqueeze(2)
                                            .to_broadcast([P, NC, P]), ALU.mult).then_inc(et_done, 1)

                def step(name, k, h, b):
                    if name == "scores":
                        masked(0, h)
                        masked(1, h)
                    if name == "level" and k + 2 <= NL:
                        masked(k + 2, h)
                    if name == "read" and k == 2 and not (isinstance(h, int) and h == NH - 1):
                        prepare(h + 1, 1 - b)
                    if name == "solve" and k == STATS_CHUNK and not (isinstance(h, int) and h == NH - 1):
                        weigh(h + 1, 1 - b)

                def masked(lv, h):
                    for a in range(2):
                        if lv == 0:
                            pool.wait_ge(gt_done, 2 * h + a + 1)
                        if lv == 2:
                            pool.wait_ge(xt_first, 2 * h + a + 1)
                        if lv >= 3:
                            pool.wait_ge(z_done, 2 * NL * h + 2 * (lv - 3) + a + 1)
                        nc.gpsimd.tensor_tensor(lm[lv % 2][a], gt[:, 4 * a:4 * a + 4, :],
                                                masks[:, lv, :].unsqueeze(1).to_broadcast([P, 4, P]),
                                                ALU.mult).then_inc(lm_done, 1)

                def slot(h, b, n0, ends):
                    for s, (name, k, _) in enumerate(STEPS):
                        step(name, k, h, b)
                        for j in ends[s]:
                            split(j, n0 + j + 2)

                for j in range(1, QKVZ - 1):
                    split(j, j + 2)
                prepare(0, 0)
                split(QKVZ - 1, QKVZ + 1)
                weigh(0, 0)
                slot(0, 0, QKVZ, DN_DONE)
                with pool.Fori(0, (NH - 2) // 2) as p:
                    slot(2 * p + 1, 1, QKVZ * (2 * p + 2), DN_DONE)
                    slot(2 * p + 2, 0, QKVZ * (2 * p + 3), DN_DONE)
                slot(NH - 1, 1, DN_BLOCKS, LRU_DONE)

                def lru(l, b, more=True):
                    mix(l - 1, 1 - b)
                    for j in range(2):
                        if more:
                            split(j, DN_BLOCKS + 2 * l + j + 2)

                def mix(l, b):
                    pool.wait_ge(lru_act, LA * l + 2)
                    nc.gpsimd.tensor_tensor(qkv[b][2][:], qkv[b][2][:], qkv[b][0][:], ALU.mult).then_inc(lru_ix, 1)

                def out_split(i):
                    pool.wait_ge(hi_split, N_BLOCKS + i + 1)
                    nc.gpsimd.tensor_tensor(hT_lo[:, i, :], flat(w_raw[i % 2]), hT_hi[:, i, :].bitcast(F32),
                                            ALU.subtract).then_inc(lo_split, 1)

                with pool.Fori(0, (NH - 2) // 2) as p:
                    lru(2 * p + 1, 1)
                    lru(2 * p + 2, 0)
                lru(NH - 1, 1, False)
                out_split(0)
                mix(NH - 1, 1)
                for i in range(1, QUARTER):
                    out_split(i)

            @block.scalar
            def _(act):
                def split(j, n, count, used):
                    act.wait_ge(w_loaded[j % 2], count)
                    if used:
                        act.wait_ge(projected, n - 1)
                        act.wait_ge(lo_split, n - 1)
                    nc.scalar.activation(w_hi[j % 2][:], w_raw[j % 2][:], ACT.Copy).then_inc(hi_split, 1)

                def first_tap(j, h, b):
                    act.wait_ge(projected, QKVZ * h + j + 1)
                    col = DN_TAP + (TAPS - 1) * 3 * NH + j * NH
                    nc.scalar.activation(qkv[b][j][:], pp[j % 2][:], ACT.Copy,
                                         scale=par[:, bass.ds(col + h, 1)]).then_inc(tap_first, 1)

                def silu(j, h, b):
                    act.wait_ge(tapped, 3 * (3 * h + j + 1))
                    nc.scalar.activation(qkv[b][j][:], qkv[b][j][:], ACT.Silu).then_inc(gated, 1)

                def silu_z(h):
                    act.wait_ge(projected, QKVZ * h + QKVZ)
                    nc.scalar.activation(yT[:, bass.ds(NH + h, 1), :], pp[1][:].rearrange("p (o s) -> p o s", o=1),
                                         ACT.Silu).then_inc(gated, 1)

                def ended(j, h, b, split_done=False):
                    n = QKVZ * h + j
                    if split_done:
                        pass
                    elif j < 2:
                        split(j, n + 2, 16 * (2 * h + 2), True)
                    else:
                        split(j, n + 2, 16 * (2 * h + 3), True)
                    if j < 3:
                        first_tap(j, h, b)
                    else:
                        silu_z(h)

                def lru_split(l, j):
                    split(j, DN_BLOCKS + 2 * l + j, 16 * (DN_BLOCKS // 2 + l + 1), True)

                def lru_tap(l, b):
                    act.wait_ge(projected, DN_BLOCKS + 2 * l + 1)
                    nc.scalar.activation(qkv[b][0][:], pp[0][:], ACT.Identity,
                                         scale=par[:, bass.ds(LRU_TAP + (TAPS - 1) * NH + l, 1)],
                                         bias=par[:, bass.ds(LRU_B + l, 1)]).then_inc(tap_first, 1)

                def lru_silu(l):
                    act.wait_ge(projected, DN_BLOCKS + 2 * l + 2)
                    nc.scalar.activation(yT[:, bass.ds(l, 1), :], pp[1][:].rearrange("p (o s) -> p o s", o=1),
                                         ACT.Silu).then_inc(gated, 1)

                def rows(h, b):
                    act.dma_start(ets[b][:].rearrange("p c i -> p (c i)"),
                                  gc_rows.rearrange("(h c) i -> h (c i)", h=NH)[bass.ds(h, 1), :]
                                  .to_broadcast([P, S])).then_inc(rows_in, 16)

                def decay(h, b):
                    act.wait_ge(gap_done, h + 1)
                    nc.scalar.activation(ets[b][:], ets[b][:], ACT.Relu).then_inc(decay_exp, 1)
                    act.wait_ge(decay_exp, 2 * h + 1)
                    nc.scalar.activation(ets[b][:], ets[b][:], ACT.Exp, scale=-1.0).then_inc(decay_exp, 1)

                def key_norm(h):
                    act.wait_ge(stat_step, 5 * h + 1)
                    nc.scalar.activation(small[:, 0, :], sse[:, 0, :], ACT.Sqrt).then_inc(root_n, 1)

                def out_root(h):
                    act.wait_ge(o_mean, h + 1)
                    nc.scalar.activation(small[:, 5, :], small[:, 5, :], ACT.Sqrt).then_inc(o_root, 1)

                def step(name, k, h, b, last):
                    first = isinstance(h, int) and h == 0
                    if name == "scores" and not first:
                        out_root(h - 1)
                    if name == "scores" and not last:
                        rows(h + 1, 1 - b)
                    if name == "turn":
                        for a in range(2):
                            act.wait_ge(turned, 4 * h + a + 1)
                            for c in range(4):
                                t = 4 * a + c
                                last_copy = nc.scalar.activation(kd[:, t, :], bank[a][:, c * P:(c + 1) * P],
                                                                 ACT.Copy, scale=small[:, 3, t:t + 1])
                            last_copy.then_inc(kv_ready, 1)
                    if name == "first":
                        for a in range(2):
                            act.wait_ge(x_turned, 2 * h + a + 1)
                            nc.scalar.activation(xx[a], bank[2 + a][:].rearrange("p (c i) -> p c i", i=P),
                                                 ACT.Copy).then_inc(x_first, 1)
                    if name == "read" and k == 3 and not last:
                        decay(h + 1, 1 - b)
                    if name == "solve" and k == STATS_CHUNK and not last:
                        key_norm(h + 1)
                    if name == "level":
                        zb = banks_of(k)[0:2]
                        rows_, cols = (slice(HC, P), slice(0, HC)) if k == NL - 1 else (slice(0, P), slice(0, P))
                        for a in range(2):
                            act.wait_ge(z_done, 2 * NL * h + 2 * k + a + 1)
                            nc.scalar.activation(zz[a][rows_, :, cols],
                                                 bank[zb[a]][:].rearrange("p (c i) -> p c i", i=P)[rows_, :, cols],
                                                 ACT.Copy).then_inc(z_ready, 1)
                    if name == "solve":
                        act.wait_ge(solved, NC * h + k + 1)
                        nc.scalar.activation(wsol[:], bank[2][:, 0:P], ACT.Copy).then_inc(w_ready, 1)
                        if k > 0:
                            act.wait_ge(read_done, 2 * ((NC - 1) * h + k))
                            nc.scalar.activation(o1[:], bank[1][:, 0:P], ACT.Copy,
                                                 scale=egc[:, bass.ds(h, 1), k]).then_inc(o1_ready, 1)
                    if name == "update":
                        if k > 0:
                            square(k - 1, h, b)
                    if name == "tail":
                        square(NC - 1, h, b)

                def square(c, h, b):
                    act.wait_ge(o_ready, NC * h + c + 1)
                    if c > 0:
                        act.wait_ge(o_squared, NC * h + c)
                    nc.scalar.activation(junk[:], vos[b][:, c, :], ACT.Square,
                                         accum_out=small[:, 4, c:c + 1]).then_inc(o_squared, 1)

                def slot(h, b, last=False):
                    later = []
                    for s, (name, k, _) in enumerate(STEPS):
                        step(name, k, h, b, last)
                        for j in DN_DONE[s]:
                            ended(j, h + 1, 1 - b)
                        for j in range(3):
                            if s == TAP_AT[j][-1] + 1:
                                silu(j, h + 1, 1 - b)

                rows(0, 0)
                split(1, 3, 32, True)
                for j in range(2):
                    ended(j, 0, 0, True)
                for j in range(2):
                    silu(j, 0, 0)
                ended(2, 0, 0)
                silu(2, 0, 0)
                ended(3, 0, 0)
                decay(0, 0)
                key_norm(0)
                slot(0, 0)
                with act.Fori(0, (NH - 2) // 2) as p:
                    slot(2 * p + 1, 1)
                    slot(2 * p + 2, 0)
                for s, (name, k, _) in enumerate(STEPS):
                    step(name, k, NH - 1, 1, True)
                    for j in LRU_DONE[s]:
                        lru_split(1, j)
                        if j == 0:
                            lru_tap(0, 0)
                        else:
                            lru_silu(0)
                out_root(NH - 1)

                def elementwise(l, b):
                    _, r, i = qkv[b]
                    for k, (dst, col) in enumerate(((r, LRU_BA), (i, LRU_BX))):
                        act.wait_ge(lgate_done, 2 * l + k + 1)
                        for f in range(2):
                            last = nc.scalar.activation(dst[:, HALF * f:HALF * (f + 1)], bank[2 * k + f][:],
                                                        ACT.Sigmoid, bias=par[:, bass.ds(col + l, 1)])
                        last.then_inc(lru_act, 1)
                    act.wait_ge(lru_act, LA * l + 1)
                    act.wait_ge(lru_h, l + 1)
                    nc.scalar.activation(kd[:], r[:].rearrange("p (c i) -> p c i", i=P), ACT.Tanh,
                                         scale=sp8[:, 0, bass.ds(l, 1)]).then_inc(lru_act, 1)
                    nc.scalar.activation(vos[0][:], r[:].rearrange("p (c i) -> p c i", i=P), ACT.Exp,
                                         scale=sp8[:, 1, bass.ds(l, 1)]).then_inc(lru_act, 1)
                    act.wait_ge(lru_act, LA * l + 4)
                    nc.scalar.activation(r[:].rearrange("p (c i) -> p c i", i=P), vos[0][:], ACT.Square) \
                        .then_inc(lru_act, 1)
                    act.wait_ge(lru_dve, LD * l + 1)
                    nc.scalar.activation(kd[:], kd[:], ACT.Sqrt).then_inc(lru_act, 1)

                def h_square(l, b):
                    act.wait_ge(lru_h, l + 2)
                    nc.scalar.activation(qkv[b][1][:], qkv[b][0][:], ACT.Square).then_inc(lru_act, 1)

                def norm_root(l):
                    act.wait_ge(lru_dve, LD * l + 3)
                    nc.scalar.activation(small[:, 5, :], small[:, 5, :], ACT.Sqrt).then_inc(lru_act, 1)

                def lru(l, b, more=True):
                    elementwise(l - 1, 1 - b)
                    if more:
                        lru_split(l + 1, 0)
                    lru_tap(l, b)
                    h_square(l - 1, 1 - b)
                    norm_root(l - 1)
                    if more:
                        lru_split(l + 1, 1)
                    lru_silu(l)

                with act.Fori(0, (NH - 2) // 2) as p:
                    lru(2 * p + 1, 1)
                    lru(2 * p + 2, 0)
                def out_split(i):
                    act.wait_ge(w_loaded[i % 2], 16 * (N_BLOCKS // 2 + i // 2 + 1))
                    act.wait_ge(projected, N_BLOCKS)
                    nc.scalar.activation(hT_hi[:, i, :], flat(w_raw[i % 2]), ACT.Copy).then_inc(hi_split, 1)

                lru(NH - 1, 1, False)
                out_split(0)
                elementwise(NH - 1, 1)
                out_split(1)
                out_split(2)
                h_square(NH - 1, 1)
                out_split(3)
                norm_root(NH - 1)

            @block.vector
            def _(dve):
                def tap(t, acc, src, col, count):
                    nc.vector.scalar_tensor_tensor(out=acc[:, t:], in0=src[:, 0:S - t], scalar=col, in1=acc[:, t:],
                                                   op0=ALU.mult, op1=ALU.add).then_inc(tapped, 1)

                def taps(t, j, h, b):
                    base = 3 * (3 * h + j)
                    if t == 1:
                        dve.wait_ge(tap_first, 3 * h + j + 1)
                    else:
                        dve.wait_ge(tapped, base + t - 1)
                    tap(t, qkv[b][j], pp[j % 2], par[:, bass.ds(DN_TAP + (TAPS - 1 - t) * 3 * NH + j * NH + h, 1)], 0)

                def lru_taps(l, b):
                    for t in range(1, TAPS):
                        if t == 1:
                            dve.wait_ge(tap_first, DN_CONVS + l + 1)
                        else:
                            dve.wait_ge(tapped, 3 * (DN_CONVS + l) + t - 1)
                        tap(t, qkv[b][0], pp[0], par[:, bass.ds(LRU_TAP + (TAPS - 1 - t) * NH + l, 1)], 0)

                def col(tile, h, c):
                    return tile[:, bass.ds(h, 1), c]

                def stats(h, b):
                    dve.wait_ge(stats_done, h + 1)
                    nc.vector.tensor_scalar(sse[:].rearrange("p a c -> p (a c)"), bank[3][:, 0:2 * NC], EPS, None,
                                            ALU.add).then_inc(stat_step, 1)
                    dve.wait_ge(stat_step, 5 * h + 1)
                    nc.vector.reciprocal(small[:, 1, :], sse[:, 0, :]).then_inc(stat_step, 1)
                    dve.wait_ge(stat_step, 5 * h + 2)
                    nc.vector.tensor_tensor(small[:, 2:3, :], small[:, 1:2, :], beta[:, bass.ds(h, 1), :],
                                            ALU.mult).then_inc(stat_step, 1)
                    dve.wait_ge(stat_step, 5 * h + 3)
                    nc.vector.tensor_tensor(small[:, 3:4, :], small[:, 2:3, :], ekd[:, bass.ds(h, 1), :],
                                            ALU.mult).then_inc(stat_step, 1)
                    nc.vector.tensor_scalar(qe[:, b, :], sse[:, 1, :], EPS * P, None, ALU.mult) \
                        .then_inc(stat_step, 1)

                def out_mean(h, b):
                    dve.wait_ge(o_squared, NC * (h + 1))
                    nc.vector.scalar_tensor_tensor(out=small[:, 5, :], in0=small[:, 4, :], scalar=1.0 / P,
                                                   in1=qe[:, b, :], op0=ALU.mult, op1=ALU.add).then_inc(o_mean, 1)

                def out_scale(h, b):
                    dve.wait_ge(o_root, h + 1)
                    nc.vector.reciprocal(small[:, 7, :], small[:, 5, :]).then_inc(o_rec, 1)
                    dve.wait_ge(o_rec, h + 1)
                    for a in range(2):
                        v = vos[b][:, 4 * a:4 * a + 4, :]
                        nc.vector.tensor_tensor(v, v, small[:, 7, 4 * a:4 * a + 4].unsqueeze(2)
                                                .to_broadcast([P, 4, P]), ALU.mult).then_inc(o_scaled, 1)

                def out_gate(h):
                    dve.wait_ge(gated, QKVZ * (h + 1))
                    for a in range(2):
                        dve.wait_ge(o_turned, 2 * h + a + 1)
                        y = yT[:, bass.ds(NH + h, 1), HALF * a:HALF * (a + 1)]
                        nc.vector.scalar_tensor_tensor(out=y, in0=bank[a][:].rearrange("p (o s) -> p o s", o=1),
                                                       scalar=par[:, DN_NW:DN_NW + 1], in1=y, op0=ALU.mult,
                                                       op1=ALU.mult).then_inc(y_done, 1)

                def step(name, k, h, b):
                    first = isinstance(h, int) and h == 0
                    et, vo = ets[b], vos[b]
                    if name == "scores":
                        if not first:
                            out_mean(h - 1, 1 - b)
                        dve.wait_ge(et_done, 2 * h + 2)
                        for a in range(2):
                            dve.wait_ge(scored, 4 * h + a + 1)
                            nc.vector.tensor_tensor(gt[:, 4 * a:4 * a + 4, :],
                                                    bank[a][:].rearrange("p (c i) -> p c i", i=P),
                                                    et[:, 4 * a:4 * a + 4, :], ALU.mult).then_inc(gt_done, 1)
                        for a in range(2):
                            dve.wait_ge(gt_done, 2 * h + a + 1)
                            dve.wait_ge(scored, 4 * h + a + 3)
                            nc.vector.tensor_tensor(et[:, 4 * a:4 * a + 4, :],
                                                    bank[2 + a][:].rearrange("p (c i) -> p c i", i=P),
                                                    et[:, 4 * a:4 * a + 4, :], ALU.mult).then_inc(attn_ready, 1)
                        for a in range(2):
                            dve.wait_ge(lm_done, 2 * (NL + 1) * h + a + 1)
                            nc.vector.tensor_tensor(xt[a], lm[0][a], ident[:].unsqueeze(1).to_broadcast([P, 4, P]),
                                                    ALU.add).then_inc(xt_first, 1)
                    if name == "turn":
                        dve.wait_ge(root_n, h + 1)
                        for a in range(2):
                            dve.wait_ge(turned, 4 * h + a + 3)
                            nc.vector.tensor_tensor(vo[:, 4 * a:4 * a + 4, :],
                                                    bank[2 + a][:].rearrange("p (c i) -> p c i", i=P),
                                                    small[:, 0, 4 * a:4 * a + 4].unsqueeze(2)
                                                    .to_broadcast([P, 4, P]), ALU.mult).then_inc(v_ready, 1)
                    if name == "turn" and not first:
                        out_scale(h - 1, 1 - b)
                    if name == "out" and not first:
                        out_gate(h - 1)
                    if name == "solve" and k == STATS_CHUNK and not (isinstance(h, int) and h == NH - 1):
                        stats(h + 1, 1 - b)
                    if name == "level":
                        xb = banks_of(k)[2:4]
                        for a in range(2):
                            for w, tile in enumerate((xx[a], xt[a])):
                                if k == NL - 1 and w == 0:
                                    continue
                                dve.wait_ge(x_done, 2 * NL * h + 2 * k + a + 1)
                                rows, cols = (slice(0, HC), slice(HC, P)) if k == NL - 1 else \
                                    (slice(0, P), slice(0, P))
                                tile = tile[rows, :, cols]
                                nc.vector.tensor_tensor(
                                    tile, bank[xb[a][w]][:].rearrange("p (c i) -> p c i", i=P)[rows, :, cols],
                                    tile, ALU.add).then_inc(x_up, 1)
                    if name == "read" and k > 0:
                        dve.wait_ge(read_done, 2 * ((NC - 1) * h + k - 1) + 1)
                        nc.vector.scalar_tensor_tensor(out=rhs[:], in0=bank[0][:, 0:P], scalar=col(negegc, h, k),
                                                       in1=vo[:, k, :], op0=ALU.mult, op1=ALU.add) \
                            .then_inc(rhs_ready, 1)
                    if name == "update":
                        if k < NC - 1:
                            dve.wait_ge(state_sum, (NC - 1) * h + k + 1)
                            if k == 0:
                                nc.vector.tensor_copy(state[:], bank[3][:, 0:P]).then_inc(state_ready, 1)
                            else:
                                dve.wait_ge(state_ready, (NC - 1) * h + k)
                                nc.vector.scalar_tensor_tensor(out=state[:], in0=state[:], scalar=col(eglast, h, k),
                                                               in1=bank[3][:, 0:P], op0=ALU.mult, op1=ALU.add) \
                                    .then_inc(state_ready, 1)
                        dve.wait_ge(attn_done, NC * h + k + 1)
                        if k == 0:
                            nc.vector.tensor_copy(vo[:, 0, :], bank[2][:, P:2 * P]).then_inc(o_ready, 1)
                        else:
                            dve.wait_ge(o1_ready, (NC - 1) * h + k)
                            nc.vector.tensor_tensor(vo[:, k, :], bank[2][:, P:2 * P], o1[:], ALU.add) \
                                .then_inc(o_ready, 1)
                def slot(h, b):
                    for s, (name, k, _) in enumerate(STEPS):
                        step(name, k, h, b)
                        for j in range(3):
                            if s in TAP_AT[j]:
                                taps(TAP_AT[j].index(s) + 1, j, h + 1, 1 - b)

                nc.vector.memset(seed[:, 1:2], 0.0).then_inc(lru_h, 1)
                for j in range(3):
                    for t in range(1, TAPS):
                        taps(t, j, 0, 0)
                stats(0, 0)
                slot(0, 0)
                with dve.Fori(0, (NH - 2) // 2) as p:
                    slot(2 * p + 1, 1)
                    slot(2 * p + 2, 0)
                for s, (name, k, _) in enumerate(STEPS):
                    step(name, k, NH - 1, 1)
                    for j in LRU_DONE[s]:
                        if j == 0:
                            lru_taps(0, 0)
                out_mean(NH - 1, 1)
                out_scale(NH - 1, 1)
                out_gate(NH - 1)

                def elementwise(l, b):
                    xc, r, i = qkv[b]
                    kdf, vof = (t[:].rearrange("p c i -> p (c i)") for t in (kd, vos[0]))
                    dve.wait_ge(lru_act, LA * l + 5)
                    nc.vector.scalar_tensor_tensor(out=kdf, in0=r[:], scalar=1.0, in1=kdf, op0=ALU.add,
                                                   op1=ALU.mult).then_inc(lru_dve, 1)
                    dve.wait_ge(lru_act, LA * l + 6)
                    dve.wait_ge(lru_ix, l + 1)
                    nc.vector.tensor_tensor(i[:], i[:], kdf, ALU.mult).then_inc(lru_dve, 1)
                    dve.wait_ge(lru_dve, LD * l + 2)
                    nc.vector.tensor_tensor_scan(xc[:], vof, i[:], 0.0, ALU.mult, ALU.add).then_inc(lru_h, 1)

                def norm(l, b):
                    dve.wait_ge(lstat_done, l + 1)
                    nc.vector.tensor_scalar(small[:, 5, :], bank[0][:, 0:NC], 1.0 / P, EPS, ALU.mult, ALU.add) \
                        .then_inc(lru_dve, 1)
                    dve.wait_ge(lru_act, LA * l + 8)
                    nc.vector.reciprocal(small[:, 7, :], small[:, 5, :]).then_inc(lru_dve, 1)
                    y = yT[:, bass.ds(l, 1), :]
                    dve.wait_ge(gated, DN_BLOCKS + l + 1)
                    nc.vector.scalar_tensor_tensor(out=y, in0=qkv[b][0][:].rearrange("p (o s) -> p o s", o=1),
                                                   scalar=par[:, bass.ds(LRU_NW + l, 1)], in1=y, op0=ALU.mult,
                                                   op1=ALU.mult).then_inc(lru_dve, 1)
                    dve.wait_ge(lru_dve, LD * l + 5)
                    dve.wait_ge(lcast_done, l + 1)
                    for f in range(2):
                        yf = yT[:, bass.ds(l, 1), HALF * f:HALF * (f + 1)]
                        last = nc.vector.tensor_tensor(yf, bank[2 + f][:].rearrange("p (o s) -> p o s", o=1), yf,
                                                       ALU.mult)
                    last.then_inc(lru_dve, 1)

                def lru(l, b):
                    elementwise(l - 1, 1 - b)
                    lru_taps(l, b)
                    norm(l - 1, 1 - b)

                with dve.Fori(0, (NH - 2) // 2) as p:
                    lru(2 * p + 1, 1)
                    lru(2 * p + 2, 0)
                lru(NH - 1, 1)
                elementwise(NH - 1, 1)
                norm(NH - 1, 1)

            @block.tensor
            def _(pe):
                def pieces(first, count, n0, free):
                    for q in range(first, first + count):
                        j, m0 = q // BLOCK_PIECES, q % BLOCK_PIECES * PIECE
                        if m0 == 0:
                            pe.wait_ge(lo_split, n0 + j + 1)
                            free[j]()
                        for m in range(m0, m0 + PIECE):
                            f, r = m // (PASSES * KT), m % (PASSES * KT)
                            d, n = r // PASSES, r % PASSES
                            w, hh = ((w_hi, hT_hi), (w_hi, hT_lo), (w_lo, hT_hi))[n]
                            mm = nc.tensor.matmul(pp[j % 2][:, HALF * f:HALF * (f + 1)], w[j % 2][:, d, :],
                                                  hh[:, d, HALF * f:HALF * (f + 1)], start=(r == 0),
                                                  stop=(r == PASSES * KT - 1))
                            if m == 2 * PASSES * KT - 1:
                                mm.then_inc(projected, 1)

                def dn_free(h):
                    first = isinstance(h, int) and h == 0
                    return (
                        (lambda: None) if first else (lambda: pe.wait_ge(tapped, 9 * h)),
                        (lambda: None) if first else (lambda: pe.wait_ge(gated, QKVZ * h)),
                        lambda: pe.wait_ge(tapped, 9 * h + 3),
                        lambda: pe.wait_ge(tapped, 9 * h + 6),
                    )

                def lru_free(l):
                    return (lambda: pe.wait_ge(tapped, 3 * (DN_CONVS + l)),
                            lambda: pe.wait_ge(gated, DN_BLOCKS + l))

                def step(name, k, h, b):
                    first = isinstance(h, int) and h == 0
                    qT, kT, vT = qkv[b]
                    et, vo = ets[b], vos[b]

                    def tile(t, c):
                        return t[:, c * C:(c + 1) * C]

                    if name == "stats":
                        stats(h + 1)
                    if name == "scores":
                        if not first:
                            pe.wait_ge(rhs_ready, (NC - 1) * h)
                        for a in range(4):
                            if a == 1 and not first:
                                pe.wait_ge(o1_ready, (NC - 1) * h)
                            if a == 2 and not first:
                                pe.wait_ge(o_ready, NC * h)
                            if a == 3 and first:
                                pe.wait_ge(stat_step, 1)
                            for c in range(4):
                                t = 4 * (a % 2) + c
                                mm = nc.tensor.matmul(bank[a][:, c * P:(c + 1) * P], tile(kT, t),
                                                      tile(kT if a < 2 else qT, t), start=True, stop=True)
                            mm.then_inc(scored, 1)
                    if name == "turn":
                        for a in range(4):
                            if a < 2:
                                pe.wait_ge(gt_done, 2 * h + a + 1)
                            else:
                                pe.wait_ge(attn_ready, 2 * h + a - 1)
                            if a == 2:
                                pe.wait_ge(gated, QKVZ * h + 3)
                            for c in range(4):
                                mm = nc.tensor.transpose(bank[a][:, c * P:(c + 1) * P],
                                                         tile(kT if a < 2 else vT, 4 * (a % 2) + c), ident[:])
                            mm.then_inc(turned, 1)
                    if name == "first":
                        for a in range(2):
                            pe.wait_ge(v_ready, 2 * h + a + 1)
                            pe.wait_ge(xt_first, 2 * h + a + 1)
                            for c in range(4):
                                mm = nc.tensor.transpose(bank[2 + a][:, c * P:(c + 1) * P], xt[a][:, c, :], ident[:])
                            mm.then_inc(x_turned, 1)
                    if name == "out":
                        pe.wait_ge(kv_ready, 2 * h + 2)
                        if not first:
                            out_turn(h - 1, 1 - b)
                    if name == "level":
                        zb, xb = banks_of(k)[0:2], banks_of(k)[2:4]
                        if k == 0 and not first:
                            pe.wait_ge(y_done, 2 * h)
                        for a in range(2):
                            pe.wait_ge(lm_done, 2 * (NL + 1) * h + 2 * (k + 1) + a + 1)
                            if k == 0:
                                pe.wait_ge(x_first, 2 * h + a + 1)
                            else:
                                pe.wait_ge(x_up, X_UPS * h + 4 * (k - 1) + 2 * a + 2)
                            for c in range(4):
                                if k < NL - 1 or c == 0:
                                    mm = nc.tensor.matmul(bank[zb[a]][:, c * P:(c + 1) * P],
                                                          lm[(k + 1) % 2][a][:, c, :], xx[a][:, c, :], start=True,
                                                          stop=True)
                                else:
                                    mm = nc.tensor.matmul(bank[zb[a]][HC:P, c * P:c * P + HC],
                                                          lm[(k + 1) % 2][a][0:HC, c, HC:P], xx[a][0:HC, c, 0:HC],
                                                          start=True, stop=True)
                            mm.then_inc(z_done, 1)
                        for a in range(2):
                            pe.wait_ge(z_ready, 2 * NL * h + 2 * k + a + 1)
                            if k < NL - 1:
                                for c in range(4):
                                    nc.tensor.matmul(bank[xb[a][0]][:, c * P:(c + 1) * P], xt[a][:, c, :],
                                                     zz[a][:, c, :], start=True, stop=True)
                            for c in range(4):
                                if k < NL - 1 or c == 0:
                                    mm = nc.tensor.matmul(bank[xb[a][1]][:, c * P:(c + 1) * P], zz[a][:, c, :],
                                                          xt[a][:, c, :], start=True, stop=True)
                                else:
                                    mm = nc.tensor.matmul(bank[xb[a][1]][0:HC, c * P + HC:(c + 1) * P],
                                                          zz[a][HC:P, c, 0:HC], xt[a][HC:P, c, HC:P], start=True,
                                                          stop=True)
                            mm.then_inc(x_done, 1)
                    if name == "read" and k > 0:
                        pe.wait_ge(state_ready, (NC - 1) * h + k)
                        nc.tensor.matmul(bank[0][:, 0:P], tile(kT, k), state[:], start=True, stop=True) \
                            .then_inc(read_done, 1)
                        if k > 1:
                            pe.wait_ge(o1_ready, (NC - 1) * h + k - 1)
                        nc.tensor.matmul(bank[1][:, 0:P], tile(qT, k), state[:], start=True, stop=True) \
                            .then_inc(read_done, 1)
                    if name == "solve":
                        if k == 0:
                            pe.wait_ge(x_up, X_UPS * (h + 1))
                        else:
                            pe.wait_ge(rhs_ready, (NC - 1) * h + k)
                            pe.wait_ge(o_ready, NC * h + k)
                        nc.tensor.matmul(bank[2][:, 0:P], xt[k // 4][:, k % 4, :], vo[:, 0, :] if k == 0 else rhs[:],
                                         start=True, stop=True).then_inc(solved, 1)
                    if name == "update":
                        pe.wait_ge(w_ready, NC * h + k + 1)
                        if k == STATS_CHUNK and not (isinstance(h, int) and h == NH - 1):
                            pe.wait_ge(stat_step, 5 * h + 6)
                        if k < NC - 1:
                            nc.tensor.matmul(bank[3][:, 0:P], kd[:, k, :], wsol[:], start=True, stop=True) \
                                .then_inc(state_sum, 1)
                        nc.tensor.matmul(bank[2][:, P:2 * P], et[:, k, :], wsol[:], start=True, stop=True) \
                            .then_inc(attn_done, 1)

                def stats(h):
                    for a, src in ((0, 2), (1, 3)):
                        pe.wait_ge(sq_done, 2 * h + a + 1)
                        for c in range(NC):
                            mm = nc.tensor.matmul(bank[3][:, a * NC + c:a * NC + c + 1],
                                                  yT[:, src, c * C:(c + 1) * C], ones_col, start=True, stop=True)
                    mm.then_inc(stats_done, 1)

                def out_turn(h, b):
                    for a in range(2):
                        pe.wait_ge(o_scaled, 2 * h + a + 1)
                        for c in range(4):
                            mm = nc.tensor.transpose(bank[a][:, c * P:(c + 1) * P], vos[b][:, 4 * a + c, :], ident[:])
                        mm.then_inc(o_turned, 1)

                ones_col = triu[:, P - 1:P]

                def slot(h, b):
                    done = 0
                    free = dn_free(h + 1)
                    for name, k, fill in STEPS:
                        step(name, k, h, b)
                        pieces(done, fill, QKVZ * (h + 1), free)
                        done += fill

                pieces(2 * BLOCK_PIECES, BLOCK_PIECES, 0, dn_free(0))
                stats(0)
                pieces(3 * BLOCK_PIECES, BLOCK_PIECES, 0, dn_free(0))
                slot(0, 0)
                with pe.Fori(0, (NH - 2) // 2) as p:
                    slot(2 * p + 1, 1)
                    slot(2 * p + 2, 0)
                done = 0
                for s, (name, k, fill) in enumerate(STEPS):
                    if name != "stats":
                        step(name, k, NH - 1, 1)
                    n = min(fill, 2 * BLOCK_PIECES - done)
                    if s == len(STEPS) - 1:
                        n = 2 * BLOCK_PIECES - done
                    pieces(done, n, DN_BLOCKS, lru_free(0))
                    done += n

                pe.wait_ge(o_ready, NC * NH)
                out_turn(NH - 1, 1)

                def lru_gates(l, b):
                    pe.wait_ge(tapped, 3 * (DN_CONVS + l + 1))
                    pe.wait_ge(wg_loaded[b], 16 * (l - b + 2))
                    if isinstance(l, int) and l == 0:
                        pe.wait_ge(y_done, 2 * NH)
                    else:
                        pe.wait_ge(lru_dve, LD * l - 3)
                    for k in range(2):
                        if k == 1 and not (isinstance(l, int) and l == 0):
                            pe.wait_ge(lru_dve, LD * l)
                        for f in range(2):
                            mm = nc.tensor.matmul(bank[2 * k + f][:], wg[b][:, k, :],
                                                  qkv[b][0][:, HALF * f:HALF * (f + 1)], start=True, stop=True)
                        mm.then_inc(lgate_done, 1)

                def lru_stats(l, b):
                    pe.wait_ge(lru_act, LA * l + 7)
                    for c in range(NC):
                        mm = nc.tensor.matmul(bank[0][:, c:c + 1], qkv[b][1][:, c * C:(c + 1) * C], ones_col,
                                              start=True, stop=True)
                    mm.then_inc(lstat_done, 1)

                def lru_cast(l):
                    pe.wait_ge(lru_dve, LD * l + 4)
                    for c in range(NC):
                        mm = nc.tensor.matmul(bank[2 + c // 4][:, c % 4 * P:(c % 4 + 1) * P],
                                              small[:, 7, c:c + 1].to_broadcast([P, P]), ident[:], start=True,
                                              stop=True)
                    mm.then_inc(lcast_done, 1)

                def lru(l, b):
                    n0 = DN_BLOCKS + 2 * l
                    pieces(0, BLOCK_PIECES * 3 // 2, n0, lru_free(l))
                    lru_stats(l - 1, 1 - b)
                    pieces(BLOCK_PIECES * 3 // 2, BLOCK_PIECES // 2, n0, lru_free(l))
                    lru_cast(l - 1)
                    lru_gates(l, b)

                lru_gates(0, 0)
                with pe.Fori(0, (NH - 2) // 2) as p:
                    lru(2 * p + 1, 1)
                    lru(2 * p + 2, 0)
                lru(NH - 1, 1)
                lru_stats(NH - 1, 1)
                lru_cast(NH - 1)


def output_block(nc, env, st):
    x, w_out, final_norm_w, out, yT, w_hi, w_lo = (
        env[k] for k in "x w_out final_norm_w out yT hT_hi hT_lo".split())
    NQ = 2 * D // P // QUARTER

    def sb(name, shape, dt=F32):
        return st.enter_context(nc.sbuf_tensor(name, shape, dt))

    def ps(name, shape):
        return st.enter_context(nc.psum_tensor(name, shape, F32))

    def sem(name):
        return st.enter_context(nc.semaphore(name))

    res = sb("res", [P, NC, D])
    stage = sb("stage", [P, QUARTER, D])
    y_hi = [sb(f"y_hi{i}", [P, QUARTER, P], F32R) for i in range(2)]
    y_lo = [sb(f"y_lo{i}", [P, QUARTER, P], F32R) for i in range(2)]
    fnw = sb("fnw", [P, D])
    rms = sb("rms3", [P, 3, NC])
    po = [ps(f"po{i}", [P, D]) for i in range(2)]

    x_in = [sem(f"x_in{i}") for i in range(2)]
    fnw_in = sem("fnw_in")
    stage_in = sem("stage_in")
    wo_hi = sem("wo_hi")
    wo_lo = sem("wo_lo")
    yh_done = sem("yh_done")
    yl_done = sem("yl_done")
    out_done = sem("out_done")
    added = sem("added")
    sq_done = sem("sq_done3")
    mean_done = sem("mean_done3")
    root_done = sem("root_done3")
    rec_done = sem("rec_done3")
    normed = sem("normed")
    stored = sem("stored")
    xt = x[0].rearrange("(n p) d -> p n d", p=P)
    ot = out[0].rearrange("(n p) d -> n p d", p=P)
    wv = w_out[0].rearrange("(e p) d -> p e d", p=P)

    def place(q, e):
        return QUARTER * (q % 2) + e

    def y_tile(q, t):
        return yT[:, QUARTER * q:QUARTER * (q + 1), bass.ds(t * P, P)]

    def row(t):
        return res[:, bass.ds(t, 1), :].rearrange("p o d -> p (o d)")

    with nc.Block() as block:
        @block.sync
        def _(sp):
            def load_x(i):
                n = slice(NC // 2 * i, NC // 2 * (i + 1))
                sp.dma_start(res[:, n, :], xt[:, n, :]).then_inc(x_in[i], 16)

            def load_w(q):
                sp.dma_start(stage[:], wv[:, QUARTER * q:QUARTER * (q + 1), :]).then_inc(stage_in, 16)

            load_x(0)
            load_w(1)
            load_x(1)
            sp.dma_start(fnw[:], final_norm_w.rearrange("(o d) -> o d", o=1).to_broadcast([P, D])) \
                .then_inc(fnw_in, 16)
            for q in range(2, NQ):
                sp.wait_ge(wo_lo, QUARTER * (q - 1))
                load_w(q)
            with sp.Fori(0, NC) as t:
                sp.wait_ge(normed, 2 * t + 2)
                sp.dma_start(ot[bass.ds(t, 1)].rearrange("o p d -> p (o d)"), row(t)).then_inc(stored, 16)
            sp.wait_ge(stored, 16 * NC)

        @block.scalar
        def _(act):
            def w_split(q, e):
                act.wait_ge(stage_in, 16 * q)
                if q >= 2:
                    act.wait_ge(out_done, NC * (q - 1))
                nc.scalar.activation(w_hi[:, bass.ds(place(q, e), 1), :], stage[:, bass.ds(e, 1), :], ACT.Copy) \
                    .then_inc(wo_hi, 1)

            def y_split(q, t, b):
                n = NC * q + t
                if not (isinstance(n, int) and n < 2):
                    act.wait_ge(out_done, n - 1)
                nc.scalar.activation(y_hi[b][:], y_tile(q, t), ACT.Copy).then_inc(yh_done, 1)

            def square(t):
                act.wait_ge(added, NC * (NQ - 1) + t + 1)
                nc.scalar.activation(stage[:, 0, :], row(t), ACT.Square, accum_out=rms[:, 0, bass.ds(t, 1)]) \
                    .then_inc(sq_done, 1)
                act.wait_ge(mean_done, t + 1)
                nc.scalar.activation(rms[:, 1, bass.ds(t, 1)], rms[:, 0, bass.ds(t, 1)], ACT.Sqrt) \
                    .then_inc(root_done, 1)

            for q in range(NQ):
                y_split(q, 0, 0)
                y_split(q, 1, 1)
                if q < NQ - 1:
                    y_split(q, 2, 0)
                    y_split(q, 3, 1)
                    with act.Fori(2, NC // 2) as u:
                        for b in range(2):
                            y_split(q, 2 * u + b, b)
                            w_split(q + 1, 2 * (u - 2) + b)
            act.wait_ge(wo_lo, QUARTER * (NQ - 1))
            with act.Fori(1, NC // 2) as u:
                for b in range(2):
                    y_split(NQ - 1, 2 * u + b, b)
                    square(2 * u + b - 2)
            square(NC - 2)
            square(NC - 1)

        @block.vector
        def _(dve):
            def y_split(q, t, b):
                dve.wait_ge(yh_done, NC * q + t + 1)
                nc.vector.tensor_tensor(y_lo[b][:], y_tile(q, t), y_hi[b][:].bitcast(F32), ALU.subtract) \
                    .then_inc(yl_done, 1)

            def add(q, t, b):
                dve.wait_ge(out_done, NC * q + t + 1)
                if q > 0:
                    dve.wait_ge(added, NC * (q - 1) + t + 1)
                nc.vector.tensor_tensor(row(t), po[b][:], row(t), ALU.add).then_inc(added, 1)

            def norm(t):
                dve.wait_ge(sq_done, t + 1)
                nc.vector.tensor_scalar(rms[:, 0, bass.ds(t, 1)], rms[:, 0, bass.ds(t, 1)], 1.0 / D, EPS,
                                        ALU.mult, ALU.add).then_inc(mean_done, 1)
                dve.wait_ge(root_done, t + 1)
                nc.vector.reciprocal(rms[:, 2, bass.ds(t, 1)], rms[:, 1, bass.ds(t, 1)]).then_inc(rec_done, 1)
                dve.wait_ge(rec_done, t + 1)
                nc.vector.scalar_tensor_tensor(out=row(t), in0=row(t), scalar=rms[:, 2, bass.ds(t, 1)], in1=fnw[:],
                                               op0=ALU.mult, op1=ALU.mult).then_inc(normed, 2)

            def pair(q, u):
                for b in range(2):
                    add(q, 2 * u + b - 2, b)
                    y_split(q, 2 * u + b, b)
                    if q == NQ - 1:
                        norm(2 * u + b - 2)

            for q in range(NQ):
                for b in range(2):
                    if q > 0:
                        add(q - 1, NC - 2 + b, b)
                    y_split(q, b, b)
                if q == 0:
                    dve.wait_ge(x_in[0], 16)
                    with dve.Fori(1, NC // 4 + 1) as u:
                        pair(q, u)
                    dve.wait_ge(x_in[1], 16)
                    pair(q, NC // 2 - 1)
                else:
                    if q == NQ - 1:
                        dve.wait_ge(fnw_in, 16)
                    with dve.Fori(1, NC // 2) as u:
                        pair(q, u)
            for t in (NC - 2, NC - 1):
                add(NQ - 1, t, t % 2)
                norm(t)

        @block.gpsimd
        def _(pool):
            for q in range(1, NQ):
                with pool.Fori(0, QUARTER) as e:
                    pool.wait_ge(wo_hi, QUARTER * (q - 1) + e + 1)
                    w = bass.ds(place(q, e), 1)
                    nc.gpsimd.tensor_tensor(w_lo[:, w, :], stage[:, bass.ds(e, 1), :], w_hi[:, w, :].bitcast(F32),
                                            ALU.subtract).then_inc(wo_lo, 1)

        @block.tensor
        def _(pe):
            def tile(q, t, b):
                n = NC * q + t
                pe.wait_ge(yl_done, n + 1)
                if not (isinstance(n, int) and n < 2):
                    pe.wait_ge(added, n - 1)
                for f in range(2):
                    cols = slice(HALF * f, HALF * (f + 1))
                    for k, (a, w) in enumerate(((y_hi, w_hi), (y_hi, w_lo), (y_lo, w_hi))):
                        for e in range(QUARTER):
                            mm = nc.tensor.matmul(po[b][:, cols], a[b][:, e, :], w[:, place(q, e), cols],
                                                  start=(k == 0 and e == 0),
                                                  stop=(k == PASSES - 1 and e == QUARTER - 1))
                mm.then_inc(out_done, 1)

            for q in range(NQ):
                if q > 0:
                    pe.wait_ge(wo_lo, QUARTER * q)
                tile(q, 0, 0)
                tile(q, 1, 1)
                with pe.Fori(1, NC // 2) as u:
                    tile(q, 2 * u, 0)
                    tile(q, 2 * u + 1, 1)


_INS = ['x', 'norm_w', 'w_in', 'lru_conv_w', 'lru_conv_b', 'lru_wa', 'lru_ba', 'lru_wx', 'lru_bx', 'lru_lambda',
        'lru_norm_w', 'dn_conv_w', 'dn_A_log', 'dn_dt_bias', 'dn_norm_w', 'w_out', 'final_norm_w']


def kernel(**inputs):
    import numpy as _np
    import concourse.bacc as _bacc
    from concourse import mybir as _mybir
    from concourse.bass_utils import run_bass_kernel_spmd as _run

    nc = _bacc.Bacc("TRN2", target_bir_lowering=False, num_devices=1)
    arrays, args = {}, []
    for name in _INS:
        a = _np.ascontiguousarray(inputs[name])
        arrays[f"in_{name}_dram"] = a
        args.append(nc.dram_tensor(f"in_{name}_dram", a.shape, _mybir.dt.from_np(a.dtype), kind="ExternalInput").ap())
    args.append(nc.dram_tensor("out_0_dram", (1, S, D), _mybir.dt.float32, kind="ExternalOutput").ap())
    build(nc, *args)
    r = _run(nc, [arrays], core_ids=[0])
    return r.results[0]["out_0_dram"]
```
